# Optimizing a Trainium2 kernel written in Bass

```python
import jax, jax.numpy as jnp
from jax import lax
import numpy as np

D_MODEL = 1024
BATCH = 1
SEQ = 512
DEPTH = 2
DEC_BATCH = 8
DEC_SEQ = 4
PAST_LEN = 4096
PAGE_SIZE = 128

N_A_LAYERS = DEPTH // 2
N_B_LAYERS = DEPTH - N_A_LAYERS
N_DENSE = (DEPTH + 1) // 2
N_MOE = DEPTH // 2

C_CONV = 3 * D_MODEL // 4
CONV_WIDTH = 31
MEM_LEN = 256
MEM_HEADS = 4
MEM_HEAD_DIM = 64
MEM_WIDTH = MEM_HEADS * MEM_HEAD_DIM
HEAD_DIM = 64
NSA_HEADS = 12
NSA_KV_HEADS = 4
HEADS_PER_GROUP = NSA_HEADS // NSA_KV_HEADS
NSA_WIDTH = NSA_HEADS * HEAD_DIM
N_BRANCH = 3
CMP_BLOCK = 32
CMP_STRIDE = 16
CMP_HIDDEN = 64
SEL_BLOCK = 64
SEL_TOP_N = 16
CHUNKS_PER_SEL = SEL_BLOCK // CMP_STRIDE
WINDOW = 512
SEL_Q_BLOCK = 32
WIN_Q_BLOCK = 128
FORCE_SCORE = 1e4
A_IN = 2 * C_CONV + MEM_WIDTH
B_IN = NSA_WIDTH + N_BRANCH * NSA_HEADS + MEM_WIDTH
MIX_WIDTH = C_CONV + MEM_WIDTH
D_FF = 2816
N_EXPERTS = 8
TOP_K = 2
D_EXPERT = 1408
MOE_BLOCK = 128
EPS = 1e-6
ATTN_SCALE = HEAD_DIM ** -0.5
MEM_SCALE = MEM_HEAD_DIM ** -0.5

kernel_name = 'yoco_conformer_nsa_decoder_step'

def rmsnorm(x, g):
    xf = x.astype(jnp.float32)
    y = xf * lax.rsqrt(jnp.mean(xf * xf, axis=-1, keepdims=True) + EPS)
    return (y * g.astype(jnp.float32)).astype(x.dtype)

def layernorm(x, g, b):
    xf = x.astype(jnp.float32)
    mu = jnp.mean(xf, axis=-1, keepdims=True)
    var = jnp.mean(jnp.square(xf - mu), axis=-1, keepdims=True)
    y = (xf - mu) * lax.rsqrt(var + EPS) * g.astype(jnp.float32) + b.astype(jnp.float32)
    return y.astype(x.dtype)

def masked_softmax(s, mask):
    s = jnp.where(mask, s.astype(jnp.float32), -jnp.inf)
    m = jnp.max(s, axis=-1, keepdims=True)
    m = jnp.where(jnp.isfinite(m), m, 0.0)
    p = jnp.exp(s - m)
    return p / jnp.maximum(jnp.sum(p, axis=-1, keepdims=True), 1e-30)

def swiglu(x, wg, wu, wd):
    return (jax.nn.silu(x @ wg) * (x @ wu)) @ wd

def moe_swiglu(x, w_router, b_router, w_gate, w_up, w_down):
    N = x.shape[0]
    NK = N * TOP_K
    logits = (x @ w_router).astype(jnp.float32) + b_router.astype(jnp.float32)
    top_val, top_idx = lax.top_k(logits, TOP_K)
    gate = jax.nn.softmax(top_val, axis=-1).astype(x.dtype)
    e_flat = top_idx.reshape(NK)
    tok_flat = jnp.repeat(jnp.arange(N, dtype=jnp.int32), TOP_K)
    g_flat = gate.reshape(NK)
    order = jnp.argsort(e_flat)
    e_s, tok_s, g_s = e_flat[order], tok_flat[order], g_flat[order]
    counts = jnp.bincount(e_flat, length=N_EXPERTS)
    starts = jnp.cumsum(counts) - counts
    padded = (counts + MOE_BLOCK - 1) // MOE_BLOCK * MOE_BLOCK
    pad_ends = jnp.cumsum(padded)
    pad_starts = pad_ends - padded
    dest = pad_starts[e_s] + jnp.arange(NK) - starts[e_s]
    n_blocks = -(-NK // MOE_BLOCK) + N_EXPERTS
    slot_tok = jnp.full((n_blocks * MOE_BLOCK,), N, jnp.int32).at[dest].set(tok_s)
    block_expert = jnp.minimum(jnp.searchsorted(pad_ends, jnp.arange(n_blocks) * MOE_BLOCK, side='right'), N_EXPERTS - 1)
    x_pad = jnp.concatenate([x, jnp.zeros((1, x.shape[1]), x.dtype)], axis=0)

    def expert_block(args):
        toks, e = args
        xb = x_pad[toks]
        return (jax.nn.silu(xb @ w_gate[e]) * (xb @ w_up[e])) @ w_down[e]

    y_slots = lax.map(expert_block, (slot_tok.reshape(n_blocks, MOE_BLOCK), block_expert))
    y_slots = y_slots.reshape(n_blocks * MOE_BLOCK, -1)
    return jax.ops.segment_sum(y_slots[dest] * g_s[:, None], tok_s, num_segments=N)

def conv_module(a, gate, prev, conv_w, conv_b, ln_g, ln_b):
    u = a * jax.nn.sigmoid(gate)
    up = jnp.concatenate([prev, u], axis=1)
    y = lax.conv_general_dilated(up, conv_w[:, None, :], window_strides=(1,), padding='VALID',
                                 dimension_numbers=('NWC', 'WIO', 'NWC'), feature_group_count=C_CONV) + conv_b
    y = jax.nn.silu(layernorm(y, ln_g, ln_b))
    return y, up[:, -(CONV_WIDTH - 1):]

def memory_kv(mem, g, w):
    B, M, _ = mem.shape
    kv = rmsnorm(mem, g) @ w
    k = kv[..., :MEM_WIDTH].reshape(B, M, MEM_HEADS, MEM_HEAD_DIM)
    v = kv[..., MEM_WIDTH:].reshape(B, M, MEM_HEADS, MEM_HEAD_DIM)
    return k, v

def memory_attend(q, k, v):
    B, T = q.shape[:2]
    s = jnp.einsum('bthd,bmhd->bhtm', q, k).astype(jnp.float32) * MEM_SCALE
    p = jax.nn.softmax(s, axis=-1).astype(v.dtype)
    return jnp.einsum('bhtm,bmhd->bthd', p, v).reshape(B, T, MEM_WIDTH)

def shared_kv(h, g, w):
    B, T, _ = h.shape
    kv = (rmsnorm(h, g) @ w).reshape(B, T, 2 * N_BRANCH, NSA_KV_HEADS, HEAD_DIM)
    return tuple(kv[:, :, i] for i in range(2 * N_BRANCH))

def chunk_proj(seq, w1):
    B, L = seq.shape[:2]
    ch = seq.reshape(B, L // CMP_STRIDE, CMP_STRIDE, NSA_KV_HEADS, HEAD_DIM)
    lo = jnp.einsum('bncgd,cdh->bngh', ch, w1[:CMP_STRIDE])
    hi = jnp.einsum('bncgd,cdh->bngh', ch, w1[CMP_STRIDE:])
    return lo, hi

def compress(segments, pe, w1, w2):
    parts = [chunk_proj(s, w1) for s in segments]
    lo = jnp.concatenate([p[0] for p in parts], axis=1)
    hi = jnp.concatenate([p[1] for p in parts], axis=1)
    pe_bias = jnp.einsum('cd,cdh->h', pe, w1)
    h = jax.nn.gelu(lo[:, :-1] + hi[:, 1:] + pe_bias)
    return jnp.einsum('bngh,hd->bngd', h, w2)

def cmp_attend(q, kc, vc, pos):
    ends = jnp.arange(kc.shape[1]) * CMP_STRIDE + CMP_BLOCK - 1
    mask = ends[None, :] <= pos[:, None]
    s = jnp.einsum('btgjd,bngd->bgjtn', q, kc).astype(jnp.float32) * ATTN_SCALE
    p = masked_softmax(s, mask)
    o = jnp.einsum('bgjtn,bngd->btgjd', p.astype(vc.dtype), vc)
    return o, p

def chunk_importance(p_c):
    half = 0.5 * jnp.sum(p_c, axis=2)
    return jnp.pad(half, ((0, 0), (0, 0), (0, 0), (0, 1))) + jnp.pad(half, ((0, 0), (0, 0), (0, 0), (1, 0)))

def sel_attend_prompt(q, sk, sv, idx, pos):
    B, T = q.shape[:2]
    n_sel = T // SEL_BLOCK
    k = idx.shape[-1]
    nq = T // SEL_Q_BLOCK
    kb = sk.reshape(B, n_sel, SEL_BLOCK, NSA_KV_HEADS, HEAD_DIM).transpose(0, 3, 1, 2, 4)
    vb = sv.reshape(B, n_sel, SEL_BLOCK, NSA_KV_HEADS, HEAD_DIM).transpose(0, 3, 1, 2, 4)
    bi = jnp.arange(B)[:, None, None, None]
    gi = jnp.arange(NSA_KV_HEADS)[None, :, None, None]
    qs = q.reshape(B, nq, SEL_Q_BLOCK, NSA_KV_HEADS, HEADS_PER_GROUP, HEAD_DIM).swapaxes(0, 1)
    ids = idx.reshape(B, NSA_KV_HEADS, nq, SEL_Q_BLOCK, k).transpose(2, 0, 1, 3, 4)
    ps = pos.reshape(nq, SEL_Q_BLOCK)

    def step(args):
        qb, ib, pb = args
        kg = kb[bi, gi, ib]
        vg = vb[bi, gi, ib]
        kpos = ib[..., None] * SEL_BLOCK + jnp.arange(SEL_BLOCK)
        mask = (kpos <= pb[:, None, None]) & (ib <= (pb // SEL_BLOCK)[:, None])[..., None]
        s = jnp.einsum('bqgjd,bgqnld->bgjqnl', qb, kg).astype(jnp.float32) * ATTN_SCALE
        p = masked_softmax(s.reshape(B, NSA_KV_HEADS, HEADS_PER_GROUP, SEL_Q_BLOCK, k * SEL_BLOCK),
                           mask.reshape(B, NSA_KV_HEADS, 1, SEL_Q_BLOCK, k * SEL_BLOCK))
        p = p.reshape(B, NSA_KV_HEADS, HEADS_PER_GROUP, SEL_Q_BLOCK, k, SEL_BLOCK).astype(vg.dtype)
        return jnp.einsum('bgjqnl,bgqnld->bqgjd', p, vg)

    o = lax.map(step, (qs, ids, ps))
    return o.swapaxes(0, 1).reshape(B, T, NSA_KV_HEADS, HEADS_PER_GROUP, HEAD_DIM)

def window_attend_prompt(q, wk, wv):
    B, T = q.shape[:2]
    nb = T // WIN_Q_BLOCK
    span = WIN_Q_BLOCK + WINDOW
    kp = jnp.pad(wk, ((0, 0), (WINDOW, 0), (0, 0), (0, 0)))
    vp = jnp.pad(wv, ((0, 0), (WINDOW, 0), (0, 0), (0, 0)))
    qrel = jnp.arange(WIN_Q_BLOCK)
    krel = jnp.arange(span) - WINDOW
    rel_ok = (krel[None, :] <= qrel[:, None]) & (krel[None, :] > qrel[:, None] - WINDOW)

    def step(n):
        start = n * WIN_Q_BLOCK
        qb = lax.dynamic_slice_in_dim(q, start, WIN_Q_BLOCK, axis=1)
        kb = lax.dynamic_slice_in_dim(kp, start, span, axis=1)
        vb = lax.dynamic_slice_in_dim(vp, start, span, axis=1)
        mask = rel_ok & (start + krel >= 0)[None, :]
        s = jnp.einsum('bqgjd,bkgd->bgjqk', qb, kb).astype(jnp.float32) * ATTN_SCALE
        p = masked_softmax(s, mask).astype(vb.dtype)
        return jnp.einsum('bgjqk,bkgd->bqgjd', p, vb)

    o = lax.map(step, jnp.arange(nb))
    return o.swapaxes(0, 1).reshape(B, T, NSA_KV_HEADS, HEADS_PER_GROUP, HEAD_DIM)

def nsa_prompt(q, gates, kvs, cmp_pe, cmp_w1, cmp_w2):
    ck, cv, sk, sv, wk, wv = kvs
    B, T = q.shape[:2]
    pos = jnp.arange(T)
    kc = compress((ck,), cmp_pe[0], cmp_w1[0], cmp_w2[0])
    vc = compress((cv,), cmp_pe[1], cmp_w1[1], cmp_w2[1])
    o_c, p_c = cmp_attend(q, kc, vc, pos)
    n_sel = T // SEL_BLOCK
    score = chunk_importance(p_c).reshape(B, NSA_KV_HEADS, T, n_sel, CHUNKS_PER_SEL).sum(-1)
    cur = (pos // SEL_BLOCK)[:, None]
    j = jnp.arange(n_sel)[None, :]
    forced = (j == 0) | (j == cur) | (j == cur - 1)
    score = jnp.where(forced, FORCE_SCORE, jnp.where(j <= cur, score, -jnp.inf))
    _, idx = lax.top_k(score, min(SEL_TOP_N, n_sel))
    o_s = sel_attend_prompt(q, sk, sv, idx, pos)
    o_w = window_attend_prompt(q, wk, wv)
    return gates[..., 0:1] * o_c + gates[..., 1:2] * o_s + gates[..., 2:3] * o_w

def sel_attend_sample(q, sk, sv, idx, pool_k, pool_v, page_table):
    B, S = q.shape[:2]
    k = idx.shape[-1]
    blocks_per_page = PAGE_SIZE // SEL_BLOCK
    bi = jnp.arange(B)[:, None, None, None]
    phys = page_table[bi, idx // blocks_per_page][..., None]
    rows = (idx % blocks_per_page)[..., None] * SEL_BLOCK + jnp.arange(SEL_BLOCK)
    gi = jnp.arange(NSA_KV_HEADS)[None, :, None, None, None]
    kg = pool_k[phys, rows, gi]
    vg = pool_v[phys, rows, gi]
    s_past = jnp.einsum('bsgjd,bgsnld->bgjsnl', q, kg).reshape(B, NSA_KV_HEADS, HEADS_PER_GROUP, S, k * SEL_BLOCK)
    s_new = jnp.einsum('bsgjd,brgd->bgjsr', q, sk)
    s = jnp.concatenate([s_past, s_new], axis=-1).astype(jnp.float32) * ATTN_SCALE
    causal = jnp.arange(S)[None, :] <= jnp.arange(S)[:, None]
    mask = jnp.concatenate([jnp.ones((S, k * SEL_BLOCK), bool), causal], axis=-1)
    p = masked_softmax(s, mask)
    p_past = p[..., :k * SEL_BLOCK].reshape(B, NSA_KV_HEADS, HEADS_PER_GROUP, S, k, SEL_BLOCK).astype(vg.dtype)
    p_new = p[..., k * SEL_BLOCK:].astype(sv.dtype)
    return jnp.einsum('bgjsnl,bgsnld->bsgjd', p_past, vg) + jnp.einsum('bgjsr,brgd->bsgjd', p_new, sv)

def window_attend_sample(q, wk, wv, buf_k, buf_v, pos):
    n_buf = buf_k.shape[1]
    kw = jnp.concatenate([buf_k, wk], axis=1)
    vw = jnp.concatenate([buf_v, wv], axis=1)
    kpos = PAST_LEN - n_buf + jnp.arange(kw.shape[1])
    mask = (kpos[None, :] <= pos[:, None]) & (kpos[None, :] > pos[:, None] - WINDOW)
    s = jnp.einsum('bsgjd,bkgd->bgjsk', q, kw).astype(jnp.float32) * ATTN_SCALE
    p = masked_softmax(s, mask).astype(vw.dtype)
    return jnp.einsum('bgjsk,bkgd->bsgjd', p, vw)

def nsa_sample(q, gates, kvs, cache_cmp_k, cache_cmp_v, cache_sel_k, cache_sel_v, page_table,
               state_win_k, state_win_v, cmp_pe, cmp_w1, cmp_w2):
    ck, cv, sk, sv, wk, wv = kvs
    B, S = q.shape[:2]
    pos = PAST_LEN + jnp.arange(S)
    n_full = (S // CMP_STRIDE) * CMP_STRIDE
    ck_past = cache_cmp_k[page_table].reshape(B, PAST_LEN, NSA_KV_HEADS, HEAD_DIM)
    cv_past = cache_cmp_v[page_table].reshape(B, PAST_LEN, NSA_KV_HEADS, HEAD_DIM)
    kc = compress((ck_past, ck[:, :n_full]), cmp_pe[0], cmp_w1[0], cmp_w2[0])
    vc = compress((cv_past, cv[:, :n_full]), cmp_pe[1], cmp_w1[1], cmp_w2[1])
    o_c, p_c = cmp_attend(q, kc, vc, pos)
    n_past_blk = PAST_LEN // SEL_BLOCK
    score = chunk_importance(p_c)[..., :n_past_blk * CHUNKS_PER_SEL]
    score = score.reshape(B, NSA_KV_HEADS, S, n_past_blk, CHUNKS_PER_SEL).sum(-1)
    j = jnp.arange(n_past_blk)
    score = jnp.where((j == 0) | (j == n_past_blk - 1), FORCE_SCORE, score)
    _, idx = lax.top_k(score, min(SEL_TOP_N - 1, n_past_blk))
    o_s = sel_attend_sample(q, sk, sv, idx, cache_sel_k, cache_sel_v, page_table)
    o_w = window_attend_sample(q, wk, wv, state_win_k, state_win_v, pos)
    return gates[..., 0:1] * o_c + gates[..., 1:2] * o_s + gates[..., 2:3] * o_w

def setup_inputs(seed: int = 0) -> dict:
    key = jax.random.key(seed)
    ks = iter(jax.random.split(key, 48))

    def nrm(shape, scale=1.0):
        return jax.random.normal(next(ks), shape, jnp.float32) * scale

    def gain(shape):
        return 1.0 + nrm(shape, 0.02)

    n_pages = PAST_LEN // PAGE_SIZE
    n_phys = (DEC_BATCH * n_pages * 5) // 4
    win_buf = min(WINDOW, PAST_LEN)
    G, HD, D = NSA_KV_HEADS, HEAD_DIM, D_MODEL
    inp = {}
    inp['x_prompt'] = nrm((BATCH, SEQ, D))
    inp['x_sample'] = nrm((DEC_BATCH, DEC_SEQ, D))
    inp['cache_mem_k'] = nrm((DEPTH, DEC_BATCH, MEM_LEN, MEM_HEADS, MEM_HEAD_DIM))
    inp['cache_mem_v'] = nrm((DEPTH, DEC_BATCH, MEM_LEN, MEM_HEADS, MEM_HEAD_DIM))
    inp['state_conv'] = nrm((N_A_LAYERS, DEC_BATCH, CONV_WIDTH - 1, C_CONV), 0.5)
    inp['cache_cmp_k'] = nrm((n_phys, PAGE_SIZE, G, HD))
    inp['cache_cmp_v'] = nrm((n_phys, PAGE_SIZE, G, HD))
    inp['cache_sel_k'] = nrm((n_phys, PAGE_SIZE, G, HD))
    inp['cache_sel_v'] = nrm((n_phys, PAGE_SIZE, G, HD))
    inp['state_win_k'] = nrm((DEC_BATCH, win_buf, G, HD))
    inp['state_win_v'] = nrm((DEC_BATCH, win_buf, G, HD))
    inp['page_table'] = jax.random.permutation(next(ks), n_phys)[:DEC_BATCH * n_pages].reshape(DEC_BATCH, n_pages).astype(jnp.int32)
    inp['mem_prompt'] = nrm((BATCH, MEM_LEN, D))
    inp['g_mix'] = gain((DEPTH, D))
    inp['g_ffn'] = gain((DEPTH, D))
    inp['g_mem'] = gain((DEPTH, D))
    inp['w_mem_kv'] = nrm((DEPTH, D, 2 * MEM_WIDTH), D ** -0.5)
    inp['w_in_a'] = nrm((N_A_LAYERS, D, A_IN), D ** -0.5)
    inp['conv_w'] = nrm((N_A_LAYERS, CONV_WIDTH, C_CONV), CONV_WIDTH ** -0.5)
    inp['conv_b'] = nrm((N_A_LAYERS, C_CONV), 0.02)
    inp['ln_g'] = gain((N_A_LAYERS, C_CONV))
    inp['ln_b'] = nrm((N_A_LAYERS, C_CONV), 0.02)
    inp['w_in_b'] = nrm((N_B_LAYERS, D, B_IN), D ** -0.5)
    inp['g_kv'] = gain((D,))
    inp['w_kv'] = nrm((D, 2 * N_BRANCH * G * HD), D ** -0.5)
    inp['cmp_pe'] = nrm((2, CMP_BLOCK, HD), 0.1)
    inp['cmp_w1'] = nrm((2, CMP_BLOCK, HD, CMP_HIDDEN), (CMP_BLOCK * HD) ** -0.5)
    inp['cmp_w2'] = nrm((2, CMP_HIDDEN, HD), CMP_HIDDEN ** -0.5)
    inp['w_out'] = nrm((DEPTH, MIX_WIDTH, D), MIX_WIDTH ** -0.5)
    inp['w_ff_gate'] = nrm((N_DENSE, D, D_FF), D ** -0.5)
    inp['w_ff_up'] = nrm((N_DENSE, D, D_FF), D ** -0.5)
    inp['w_ff_down'] = nrm((N_DENSE, D_FF, D), D_FF ** -0.5)
    inp['w_router'] = nrm((N_MOE, D, N_EXPERTS), D ** -0.5)
    inp['b_router'] = nrm((N_MOE, N_EXPERTS), 0.01)
    inp['w_e_gate'] = nrm((N_MOE, N_EXPERTS, D, D_EXPERT), D ** -0.5)
    inp['w_e_up'] = nrm((N_MOE, N_EXPERTS, D, D_EXPERT), D ** -0.5)
    inp['w_e_down'] = nrm((N_MOE, N_EXPERTS, D_EXPERT, D), D_EXPERT ** -0.5)
    inp['g_final'] = gain((D,))
    return inp

def reference(x_prompt, x_sample, cache_mem_k, cache_mem_v, state_conv, cache_cmp_k, cache_cmp_v,
              cache_sel_k, cache_sel_v, state_win_k, state_win_v, page_table, mem_prompt,
              g_mix, g_ffn, g_mem, w_mem_kv, w_in_a, conv_w, conv_b, ln_g, ln_b, w_in_b, g_kv, w_kv,
              cmp_pe, cmp_w1, cmp_w2, w_out, w_ff_gate, w_ff_up, w_ff_down, w_router, b_router,
              w_e_gate, w_e_up, w_e_down, g_final):

    def channel_mixer(h, l):
        B, T, _ = h.shape
        hn = rmsnorm(h, g_ffn[l])
        i = l // 2
        if l % 2 == 0:
            y = swiglu(hn, w_ff_gate[i], w_ff_up[i], w_ff_down[i])
        else:
            y = moe_swiglu(hn.reshape(B * T, D_MODEL), w_router[i], b_router[i],
                           w_e_gate[i], w_e_up[i], w_e_down[i]).reshape(B, T, D_MODEL)
        return h + y

    def run_group(x, conv_prev, mem_k, mem_v, nsa_branch):
        B, T, _ = x.shape
        h = x
        conv_tails = []
        shared = None
        for l in range(DEPTH):
            hn = rmsnorm(h, g_mix[l])
            if l < N_A_LAYERS:
                z = hn @ w_in_a[l]
                tok, tail = conv_module(z[..., :C_CONV], z[..., C_CONV:2 * C_CONV], conv_prev[l],
                                        conv_w[l], conv_b[l], ln_g[l], ln_b[l])
                conv_tails.append(tail)
                q_mem = z[..., 2 * C_CONV:]
            else:
                if shared is None:
                    shared = shared_kv(h, g_kv, w_kv)
                z = hn @ w_in_b[l - N_A_LAYERS]
                q = z[..., :NSA_WIDTH].reshape(B, T, NSA_KV_HEADS, HEADS_PER_GROUP, HEAD_DIM)
                gates = jax.nn.sigmoid(z[..., NSA_WIDTH:NSA_WIDTH + N_BRANCH * NSA_HEADS]).reshape(
                    B, T, NSA_KV_HEADS, HEADS_PER_GROUP, N_BRANCH)
                tok = nsa_branch(q, gates, shared).reshape(B, T, NSA_WIDTH)
                q_mem = z[..., NSA_WIDTH + N_BRANCH * NSA_HEADS:]
            mem_o = memory_attend(q_mem.reshape(B, T, MEM_HEADS, MEM_HEAD_DIM), mem_k[l], mem_v[l])
            h = h + jnp.concatenate([tok, mem_o], axis=-1) @ w_out[l]
            h = channel_mixer(h, l)
        return rmsnorm(h, g_final), jnp.stack(conv_tails), shared

    mem_kv_p = [memory_kv(mem_prompt, g_mem[l], w_mem_kv[l]) for l in range(DEPTH)]
    mem_k_p = jnp.stack([kv[0] for kv in mem_kv_p])
    mem_v_p = jnp.stack([kv[1] for kv in mem_kv_p])
    conv_zero = jnp.zeros((N_A_LAYERS, x_prompt.shape[0], CONV_WIDTH - 1, C_CONV), x_prompt.dtype)

    def nsa_p(q, g, kv):
        return nsa_prompt(q, g, kv, cmp_pe, cmp_w1, cmp_w2)

    def nsa_s(q, g, kv):
        return nsa_sample(q, g, kv, cache_cmp_k, cache_cmp_v, cache_sel_k, cache_sel_v, page_table,
                          state_win_k, state_win_v, cmp_pe, cmp_w1, cmp_w2)

    y_prompt, conv_p, kv_p = run_group(x_prompt, conv_zero, mem_k_p, mem_v_p, nsa_p)
    y_sample, conv_s, kv_s = run_group(x_sample, state_conv, cache_mem_k, cache_mem_v, nsa_s)

    keep_p = min(WINDOW, x_prompt.shape[1])
    win_k_p = kv_p[4][:, -keep_p:]
    win_v_p = kv_p[5][:, -keep_p:]
    keep_s = min(WINDOW, state_win_k.shape[1] + x_sample.shape[1])
    win_k_s = jnp.concatenate([state_win_k, kv_s[4]], axis=1)[:, -keep_s:]
    win_v_s = jnp.concatenate([state_win_v, kv_s[5]], axis=1)[:, -keep_s:]
    return (y_prompt, y_sample, mem_k_p, mem_v_p, conv_p, conv_s,
            kv_p[0], kv_p[1], kv_p[2], kv_p[3], kv_s[0], kv_s[1], kv_s[2], kv_s[3],
            win_k_p, win_v_p, win_k_s, win_v_s)


_drawn_inputs = setup_inputs


def setup_inputs(seed=0):
    import zlib

    import numpy as np

    out = dict(_drawn_inputs(seed))
    spreads = {}
    factors = {'g_mem': 2.752,
     'g_kv': 2.87,
     'g_final': 7.409,
     'cache_cmp_k': 3.047,
     'cache_cmp_v': 3.309,
     'cache_sel_k': 3.759,
     'cache_sel_v': 2.989,
     'b_router': 5.1}
    for name, (base, spread) in spreads.items():
        noise = np.random.default_rng([zlib.crc32(name.encode()), seed]).standard_normal(out[name].shape)
        drawn = base * np.exp(spread * noise) if base else spread * noise
        out[name] = __import__('jax').numpy.asarray(drawn.astype(out[name].dtype))
    for name, factor in factors.items():
        out[name] = (out[name] * factor).astype(out[name].dtype)
    return out
```

```python
from contextlib import ExitStack

import concourse.bass as bass
from concourse import mybir

P = 128
F32 = mybir.dt.float32
I32 = mybir.dt.int32
U32 = mybir.dt.uint32
ALU = mybir.AluOpType
ACT = mybir.ActivationFunctionType
AX_X = mybir.AxisListType.X
ds = bass.ds

D = 1024
KD = D // P
TP, DB, DS = 512, 8, 4
TS = DB * DS
T = TP + TS
HALF = T // 2
NT = TP // P
CONV, CW = 768, 31
KC = CONV // P
TAIL = CW - 1
MEM = 256
NH, NG, NJ, HD = 12, 4, 3, 64
GW = NG * HD
DFF, DEX, NE = 2816, 1408, 8
PAST, PAGE, NPHYS = 4096, 128, 320
WIN = 512
CH = 16
NCH = PAST // CH
SELB, NSEL = 64, PAST // 64
EPS = 1e-6
SCALE = HD ** -0.5
NEG = -1e30
FORCE = 1e4

VEC = {}
_row = 0
for _name, _len in (("g_mix", 16), ("g_ffn", 16), ("g_mem", 16), ("g_kv", 8), ("g_final", 8),
                    ("conv_b", 6), ("ln_g", 6), ("ln_b", 6)):
    VEC[_name] = (_row, _len)
    _row += _len
NVEC = _row


class Stage:

    def __init__(self, nc, name):
        self.nc, self.name = nc, name
        self.ctx, self.sems, self.pool_dma = ExitStack(), [], False

    def sb(self, name, shape, dt=F32):
        return self.ctx.enter_context(self.nc.sbuf_tensor(f"{self.name}_{name}", shape, dt))

    def sem(self, name):
        s = self.ctx.enter_context(self.nc.semaphore(f"{self.name}_{name}"))
        self.sems.append(s)
        return s

    def open(self):
        self.guard = self.nc.Block(no_gpsimd_drain=True)
        return self.guard.__enter__()

    def __enter__(self):
        return self

    def close(self):
        self.guard.__exit__(None, None, None)
        with self.nc.Block(no_gpsimd_drain=True) as block:
            if self.pool_dma:
                @block.gpsimd
                def _(pool):
                    pool.dma_reset()
                    for s in self.sems:
                        pool.sem_clear(s)
            else:
                @block.sync
                def _(sp):
                    for s in self.sems:
                        sp.sem_clear(s)

    def __exit__(self, kind, value, trace):
        if kind is None:
            self.close()
            self.ctx.close()
        return False


class Core:

    def __init__(self, nc, ctx):
        self.nc, self.ctx = nc, ctx
        self.banks = ctx.enter_context(nc.psum_tensor("banks", [P, 8, 512], F32))
        self.ps = [self.banks[:, i, :] for i in range(8)]
        self.ident = self.sb("ident", [P, P])
        self.mean_d = self.sb("mean_d", [P, P])
        self.mean_c = self.sb("mean_c", [P, P])
        self.vec = self.sb("vec", [P, NVEC])
        self.eps = self.sb("eps", [P, 1])
        self.hT = self.sb("hT", [P, KD, T])

    def sb(self, name, shape, dt=F32):
        return self.ctx.enter_context(self.nc.sbuf_tensor(name, shape, dt))

    def col(self, name, k):
        return self.vec[:, VEC[name][0] + k:VEC[name][0] + k + 1]


def halves(n):
    return [(0, HALF), (HALF, HALF)] if n == T else [(0, n)]



def load_tokens(nc, core, A):
    with Stage(nc, "load") as st:
        x_nat = st.sb("x_nat", [P, NT + 1, D])
        rows = st.sb("rows", [P, P])
        consts_in, rows_in, tokens_in = st.sem("consts_in"), st.sem("rows_in"), [st.sem(f"tokens_in{t}") for t in range(NT + 1)]
        turned, copied = st.sem("turned"), st.sem("copied")
        block = st.open()
        groups = [(t, k0) for t in range(NT + 1) for k0 in (0, 4)]

        @block.sync
        def _(sp):
            sp.dma_start(core.ident[:, :], A["c_ident"]).then_inc(consts_in, 16)
            for name, (r0, n) in VEC.items():
                flat = A[name].rearrange("l d -> (l d)") if len(A[name].shape) == 2 else A[name]
                sp.dma_start(rows[r0:r0 + n, :], flat.rearrange("(r c) -> r c", c=P)).then_inc(rows_in, 16)
            for t in range(NT):
                sp.dma_start(x_nat[:, t, :], A["x_prompt"][0, t * P:(t + 1) * P, :]).then_inc(tokens_in[t], 16)
            sp.dma_start(x_nat[:TS, NT, :], A["x_sample"].rearrange("b s d -> (b s) d")).then_inc(tokens_in[NT], 16)

        @block.tensor
        def _(pe):
            pe.wait_ge(consts_in, 16)
            pe.wait_ge(rows_in, 16 * len(VEC))
            pe.transpose(core.ps[0][:, :NVEC], rows[:NVEC, :], core.ident[:NVEC, :NVEC]).then_inc(turned, 1)
            for n, (t, k0) in enumerate(groups):
                rows_t = P if t < NT else TS
                bank = core.ps[(n + 1) % 8]
                pe.wait_ge(tokens_in[t], 16)
                if n + 1 >= 8:
                    pe.wait_ge(copied, n + 1 - 8 + 1)
                for k in range(4):
                    mm = pe.transpose(bank[:, k * P:k * P + rows_t], x_nat[:rows_t, t, (k0 + k) * P:(k0 + k + 1) * P],
                                      core.ident[:rows_t, :rows_t])
                mm.then_inc(turned, 1)

        @block.vector
        def _(dve):
            dve.memset(core.eps[:, :], EPS)
            dve.memset(core.mean_d[:, :], 1.0 / D)
            dve.memset(core.mean_c[:, :], 1.0 / CONV)
            dve.wait_ge(turned, 1)
            dve.tensor_copy(core.vec[:, :], core.ps[0][:, :NVEC]).then_inc(copied, 1)
            for n, (t, k0) in enumerate(groups):
                rows_t = P if t < NT else TS
                dve.wait_ge(turned, n + 2)
                src = core.ps[(n + 1) % 8].rearrange("p (k c) -> p k c", k=4)[:, :, :rows_t]
                dve.tensor_copy(core.hT[:, k0:k0 + 4, t * P:t * P + rows_t], src).then_inc(copied, 1)


def rms_norm(nc, core, name, gain, k0, out):
    with Stage(nc, name) as st:
        squares = st.sb("squares", [P, KD, T])
        rstd = st.sb("rstd", [P, T])
        squared, summed, rooted = st.sem("squared"), st.sem("summed"), st.sem("rooted")
        block = st.open()

        @block.scalar
        def _(act):
            for k in range(KD):
                act.activation(squares[:, k, :], core.hT[:, k, :], ACT.Square).then_inc(squared, 1)
            act.wait_ge(summed, 2 * KD)
            for h, (t0, n) in enumerate(halves(T)):
                act.activation(rstd[:, t0:t0 + n], core.ps[h][:, :n], ACT.Sqrt, bias=core.eps[:, :]).then_inc(rooted, 1)

        @block.tensor
        def _(pe):
            for k in range(KD):
                pe.wait_ge(squared, k + 1)
                for h, (t0, n) in enumerate(halves(T)):
                    pe.matmul(core.ps[h][:, :n], core.mean_d[:, :], squares[:, k, t0:t0 + n],
                              start=(k == 0), stop=(k == KD - 1)).then_inc(summed, 1)

        @block.vector
        def _(dve):
            for h, (t0, n) in enumerate(halves(T)):
                dve.wait_ge(rooted, h + 1)
                dve.reciprocal(rstd[:, t0:t0 + n], rstd[:, t0:t0 + n])
            dve.drain()
            for k in range(KD):
                dve.scalar_tensor_tensor(out=out[:, k, :], in0=core.hT[:, k, :], scalar=core.col(gain, k0 + k),
                                         in1=rstd[:, :], op0=ALU.mult, op1=ALU.mult)


def memory_kv(nc, core, A, O, memv, memkT):
    MT = MEM // P
    with Stage(nc, "memkv") as st:
        nat = st.sb("nat", [P, MT, D])
        sq = st.sb("sq", [P, D])
        ss, root = st.sb("ss", [P, MT]), st.sb("root", [P, MT])
        memT = [st.sb(f"memT{l}", [P, KD, MEM]) for l in range(2)]
        w = [st.sb(f"w{l}", [P, KD, 2 * GW]) for l in range(2)]
        mem_in, w_in = st.sem("mem_in"), [st.sem(f"w_in{l}") for l in range(2)]
        squares_done, normed, turned, scaled = st.sem("squares_done"), st.sem("normed"), st.sem("turned"), st.sem("scaled")
        projected, kv_copied, k_turned, stored = st.sem("projected"), st.sem("kv_copied"), st.sem("k_turned"), st.sem("stored")
        block = st.open()

        @block.sync
        def _(sp):
            sp.dma_start(nat[:, :, :], A["mem_prompt"][0].rearrange("(m p) d -> p m d", p=P)).then_inc(mem_in, 16)
            for l in range(2):
                sp.dma_start(w[l][:, :, :], A["w_mem_kv"][l].rearrange("(k p) n -> p k n", p=P)).then_inc(w_in[l], 16)
            for l in range(2):
                for m in range(MT):
                    sp.wait_ge(kv_copied, l * MT + m + 1)
                    for i, name in enumerate(("mem_k_p", "mem_v_p")):
                        sp.dma_start(O[name][l, 0, m * P:(m + 1) * P].rearrange("m h d -> m (h d)"),
                                     memv[l][:, m, i * GW:(i + 1) * GW]).then_inc(stored, 16)
            sp.wait_ge(stored, 16 * 4 * MT)

        @block.scalar
        def _(act):
            act.wait_ge(mem_in, 16)
            for m in range(MT):
                act.activation(sq[:, :], nat[:, m, :], ACT.Square, accum_out=ss[:, m:m + 1]).then_inc(squares_done, 1)
                act.drain()
            act.activation(root[:, :], ss[:, :], ACT.Sqrt, bias=core.eps[:, :], scale=1.0 / D).then_inc(squares_done, 1)

        @block.vector
        def _(dve):
            dve.wait_ge(squares_done, MT + 1)
            dve.reciprocal(ss[:, :], root[:, :])
            dve.drain()
            for m in range(MT):
                dve.tensor_scalar(nat[:, m, :], nat[:, m, :], ss[:, m:m + 1], None, ALU.mult).then_inc(normed, 1)
            for n in range(MT * 2):
                m, k0 = n // 2, 4 * (n % 2)
                dve.wait_ge(turned, n + 1)
                for k in range(4):
                    for l in range(2):
                        dve.tensor_scalar(memT[l][:, k0 + k, m * P:(m + 1) * P], core.ps[n][:, k * P:(k + 1) * P],
                                          core.col("g_mem", l * KD + k0 + k), None, ALU.mult).then_inc(scaled, 1)
            for n in range(2 * MT):
                dve.wait_ge(projected, n + 1)
                dve.tensor_copy(memv[n // MT][:, n % MT, :], core.ps[4 + n][:, :]).then_inc(kv_copied, 1)
            for l in range(2):
                for hp in range(2):
                    dve.wait_ge(k_turned, 2 * l + hp + 1)
                    dve.tensor_copy(memkT[l][:, hp, :], core.ps[2 * l + hp][:, :MEM])

        @block.tensor
        def _(pe):
            for n in range(MT * 2):
                m, k0 = n // 2, 4 * (n % 2)
                pe.wait_ge(normed, m + 1)
                for k in range(4):
                    mm = pe.transpose(core.ps[n][:, k * P:(k + 1) * P], nat[:, m, (k0 + k) * P:(k0 + k + 1) * P], core.ident[:, :])
                mm.then_inc(turned, 1)
            pe.wait_ge(scaled, 2 * KD * MT)
            for l in range(2):
                pe.wait_ge(w_in[l], 16)
                for m in range(MT):
                    for k in range(KD):
                        mm = pe.matmul(core.ps[4 + l * MT + m][:, :], memT[l][:, k, m * P:(m + 1) * P], w[l][:, k, :],
                                       start=(k == 0), stop=(k == KD - 1))
                    mm.then_inc(projected, 1)
            for l in range(2):
                pe.wait_ge(kv_copied, MT * (l + 1))
                for hp in range(2):
                    for m in range(MT):
                        mm = pe.transpose(core.ps[2 * l + hp][:, m * P:(m + 1) * P],
                                          memv[l][:, m, hp * P:(hp + 1) * P], core.ident[:, :])
                    mm.then_inc(k_turned, 1)



def conv_input(nc, core, A, O, hn, up_p, up_s, qmT, convw):
    W = A["w_in_a"][0].rearrange("(k p) n -> p k n", p=P)
    with Stage(nc, "zin") as st:
        w = [st.sb(f"w{i}", [P, KD, 2 * P]) for i in range(2)]
        sig = [st.sb(f"sig{i}", [P, HALF]) for i in range(2)]
        prev = st.sb("prev", [120, 2, CONV])
        cw_nat = st.sb("cw_nat", [CW, CONV])
        tail = st.sb("tail", [TS, 2, CONV])
        tail_cols = st.sb("tail_cols", [P, KC, TS])
        w_in = [st.sem(f"w_in{i}") for i in range(2)]
        prev_in, prev_turned, prev_copied = st.sem("prev_in"), st.sem("prev_turned"), st.sem("prev_copied")
        sig_done = st.sem("sig_done")
        multiplied, gated, banks_free = st.sem("multiplied"), st.sem("gated"), st.sem("banks_free")
        q_done, q_copied = st.sem("q_done"), st.sem("q_copied")
        tail_turned, tail_copied, stored = st.sem("tail_turned"), st.sem("tail_copied"), st.sem("stored")
        block = st.open()

        def turned_pieces():
            for c in range(KC):
                yield c, core.ps[c]

        @block.sync
        def _(sp):
            sp.dma_start(prev[:, :, :], A["state_conv"][0].rearrange("(i b) w c -> (b w) i c", i=2)).then_inc(prev_in, 16)
            sp.dma_start(cw_nat[:, :], A["conv_w"][0]).then_inc(prev_in, 16)
            for n in range(KC):
                if n >= 2:
                    sp.wait_ge(multiplied, n - 1)
                sp.dma_start(w[n % 2][:, :, 0:P], W[:, :, n * P:(n + 1) * P]).then_inc(w_in[n % 2], 16)
                sp.dma_start(w[n % 2][:, :, P:2 * P], W[:, :, CONV + n * P:CONV + (n + 1) * P]).then_inc(w_in[n % 2], 16)
            sp.wait_ge(multiplied, KC - 1)
            sp.dma_start(w[0][:, :, :], W[:, :, 2 * CONV:]).then_inc(w_in[0], 32)
            sp.dma_start(O["conv_s"][0, :, 0:TAIL - DS, :], A["state_conv"][0, :, DS:, :]).then_inc(stored, 16)
            sp.wait_ge(tail_copied, 2 * KC)
            sp.dma_start(O["conv_p"][0, 0], tail[:TAIL, 0, :]).then_inc(stored, 16)
            for b in range(DB):
                sp.dma_start(O["conv_s"][0, b, TAIL - DS:, :], tail[b * DS:(b + 1) * DS, 1, :]).then_inc(stored, 16)
            sp.wait_ge(stored, 16 * (2 + DB))

        @block.tensor
        def _(pe):
            pe.wait_ge(prev_in, 32)
            for c, bank in turned_pieces():
                for i in range(2):
                    pe.transpose(bank[:, i * 120:(i + 1) * 120], prev[:, i, c * P:(c + 1) * P], core.ident[:120, :120])
                pe.transpose(bank[:, 240:240 + CW], cw_nat[:, c * P:(c + 1) * P],
                             core.ident[:CW, :CW]).then_inc(prev_turned, 1)
            for i in range(KC):
                pe.wait_ge(w_in[i % 2], (i // 2 + 1) * 32)
                pe.wait_ge(banks_free, max(i, 1))
                for part in range(2):
                    for h, (t0, n) in enumerate(halves(T)):
                        for k in range(KD):
                            mm = pe.matmul(core.ps[4 * (i % 2) + 2 * part + h][:, :n],
                                           w[i % 2][:, k, part * P:(part + 1) * P],
                                           hn[:, k, t0:t0 + n], start=(k == 0), stop=(k == KD - 1))
                mm.then_inc(multiplied, 1)
            pe.wait_ge(w_in[0], 32 * (KC // 2 + 1))
            pe.wait_ge(banks_free, KC)
            for m in range(2):
                for h, (t0, n) in enumerate(halves(T)):
                    for k in range(KD):
                        mm = pe.matmul(core.ps[2 * m + h][:, :n], w[0][:, k, m * P:(m + 1) * P], hn[:, k, t0:t0 + n],
                                       start=(k == 0), stop=(k == KD - 1))
            mm.then_inc(q_done, 1)
            pe.wait_ge(gated, KC)
            pe.wait_ge(banks_free, KC + 1)
            for c in range(KC):
                pe.transpose(core.ps[4 + c // 4][:TAIL, (c % 4) * P:(c % 4 + 1) * P], up_p[:, c, TP:TP + TAIL],
                             core.ident[:, :]).then_inc(tail_turned, 1)
            for c in range(KC):
                pe.transpose(core.ps[6 + c // 4][:TS, (c % 4) * P:(c % 4 + 1) * P], tail_cols[:, c, :],
                             core.ident[:, :]).then_inc(tail_turned, 1)

        @block.scalar
        def _(act):
            for n in range(KC):
                i, j = n // 2, n % 2
                act.wait_ge(multiplied, n + 1)
                if n >= 1:
                    act.wait_ge(gated, n)
                for h in range(2):
                    act.activation(sig[h][:, :], core.ps[4 * j + 2 + h][:, :HALF], ACT.Sigmoid)
                act.drain().then_inc(sig_done, 1)

        @block.vector
        def _(dve):
            dve.memset(up_p[:, :, 0:TAIL], 0.0)
            for c, bank in turned_pieces():
                dve.wait_ge(prev_turned, c + 1)
                dve.tensor_copy(up_s[:, c, :, 0:TAIL], bank[:, 0:240].rearrange("p (b w) -> p b w", w=TAIL))
                dve.tensor_copy(convw[:, c, :], bank[:, 240:240 + CW])
            dve.drain()
            dve.sem_inc(banks_free, 1)
            for n in range(KC):
                j = n % 2
                dve.wait_ge(sig_done, n + 1)
                dve.tensor_tensor(up_p[:, n, TAIL:TAIL + HALF], core.ps[4 * j][:, :HALF], sig[0][:, :], ALU.mult)
                dve.tensor_tensor(up_p[:, n, TAIL + HALF:], core.ps[4 * j + 1][:, :TP - HALF], sig[1][:, :TP - HALF], ALU.mult)
                dve.tensor_tensor(tail_cols[:, n, :], core.ps[4 * j + 1][:, TP - HALF:HALF], sig[1][:, TP - HALF:], ALU.mult)
                dve.drain().then_inc(gated, 1)
                dve.tensor_copy(up_s[:, n, :, TAIL:], tail_cols[:, n, :].rearrange("p (b s) -> p b s", s=DS))
                dve.sem_inc(banks_free, 1)
            dve.wait_ge(q_done, 1)
            for m in range(2):
                for h, (t0, n) in enumerate(halves(T)):
                    dve.tensor_copy(qmT[:, m, t0:t0 + n], core.ps[2 * m + h][:, :n])
            for g in range(2):
                dve.wait_ge(tail_turned, KC * (g + 1))
                rows = TAIL if g == 0 else TS
                for half, (c0, n) in enumerate(((0, 4 * P), (4 * P, 2 * P))):
                    dve.tensor_copy(tail[:rows, g, c0:c0 + n], core.ps[4 + 2 * g + half][:rows, :n]).then_inc(tail_copied, KC // 2)


def convolve(nc, core, up_p, up_s, convw, y):
    with Stage(nc, "conv") as st:
        block = st.open()

        @block.vector
        def _(dve):
            def sample(c):
                return y[:, c, TP:].rearrange("p (b s) -> p b s", s=DS)
            for c in range(KC):
                for out, src in ((y[:, c, :TP], up_p[:, c, 0:TP]), (sample(c), up_s[:, c, :, 0:DS])):
                    dve.tensor_scalar(out, src, convw[:, c, 0:1], core.col("conv_b", c), ALU.mult, ALU.add)
            for k in range(1, CW):
                dve.drain()
                for c in range(KC):
                    for out, src in ((y[:, c, :TP], up_p[:, c, k:k + TP]), (sample(c), up_s[:, c, :, k:k + DS])):
                        dve.scalar_tensor_tensor(out=out, in0=src, scalar=convw[:, c, k:k + 1], in1=out,
                                                 op0=ALU.mult, op1=ALU.add)


def conv_norm(nc, core, y, mixT):
    with Stage(nc, "ln") as st:
        sq = st.sb("sq", [P, KC, T])
        rstd = st.sb("rstd", [P, T])
        mean_done, centred, squared, var_done, rooted, normed = (st.sem(x) for x in ("mean_done", "centred", "squared", "var_done", "rooted", "normed"))
        block = st.open()

        @block.tensor
        def _(pe):
            for h, (t0, n) in enumerate(halves(T)):
                for c in range(KC):
                    mm = pe.matmul(core.ps[h][:, :n], core.mean_c[:, :], y[:, c, t0:t0 + n], start=(c == 0), stop=(c == KC - 1))
            mm.then_inc(mean_done, 1)
            for c in range(KC):
                pe.wait_ge(squared, c + 1)
                for h, (t0, n) in enumerate(halves(T)):
                    mm = pe.matmul(core.ps[2 + h][:, :n], core.mean_c[:, :], sq[:, c, t0:t0 + n], start=(c == 0), stop=(c == KC - 1))
            mm.then_inc(var_done, 1)

        @block.vector
        def _(dve):
            dve.wait_ge(mean_done, 1)
            for c in range(KC):
                for h, (t0, n) in enumerate(halves(T)):
                    dve.tensor_tensor(y[:, c, t0:t0 + n], y[:, c, t0:t0 + n], core.ps[h][:, :n], ALU.subtract).then_inc(centred, 1)
            for h, (t0, n) in enumerate(halves(T)):
                dve.wait_ge(rooted, h + 1)
                dve.reciprocal(rstd[:, t0:t0 + n], rstd[:, t0:t0 + n])
            dve.drain()
            for c in range(KC):
                dve.scalar_tensor_tensor(out=sq[:, c, :], in0=y[:, c, :], scalar=core.col("ln_g", c), in1=rstd[:, :],
                                         op0=ALU.mult, op1=ALU.mult).then_inc(normed, 1)

        @block.scalar
        def _(act):
            for c in range(KC):
                act.wait_ge(centred, 2 * (c + 1))
                act.activation(sq[:, c, :], y[:, c, :], ACT.Square).then_inc(squared, 1)
            act.wait_ge(var_done, 1)
            for h, (t0, n) in enumerate(halves(T)):
                act.activation(rstd[:, t0:t0 + n], core.ps[2 + h][:, :n], ACT.Sqrt, bias=core.eps[:, :]).then_inc(rooted, 1)
            for c in range(KC):
                act.wait_ge(normed, c + 1)
                act.activation(mixT[:, c, :], sq[:, c, :], ACT.Silu, bias=core.col("ln_b", c))



def add_product(nc, core, name, W, KB, xT):
    Wv = W.rearrange("(k p) n -> p k n", p=P)
    CB = 2 * P
    with Stage(nc, name) as st:
        w = [st.sb(f"w{i}", [P, KB, CB]) for i in range(2)]
        w_in, multiplied, added = [st.sem(f"w_in{i}") for i in range(2)], st.sem("multiplied"), st.sem("added")
        block = st.open()

        @block.sync
        def _(sp):
            for n in range(D // CB):
                if n >= 2:
                    sp.wait_ge(multiplied, 2 * (n - 1))
                sp.dma_start(w[n % 2][:, :, :], Wv[:, :, n * CB:(n + 1) * CB]).then_inc(w_in[n % 2], 16)

        @block.tensor
        def _(pe):
            for m in range(KD):
                n = m // 2
                if m % 2 == 0:
                    pe.wait_ge(w_in[n % 2], 16 * (n // 2 + 1))
                if m >= 4:
                    pe.wait_ge(added, m - 3)
                for h, (t0, cols) in enumerate(halves(T)):
                    for k in range(KB):
                        mm = pe.matmul(core.ps[2 * (m % 4) + h][:, :cols], w[n % 2][:, k, (m % 2) * P:(m % 2 + 1) * P],
                                       xT[:, k, t0:t0 + cols], start=(k == 0), stop=(k == KB - 1))
                mm.then_inc(multiplied, 1)

        @block.vector
        def _(dve):
            for m in range(KD):
                dve.wait_ge(multiplied, m + 1)
                dve.tensor_tensor(core.hT[:, m, 0:HALF], core.ps[2 * (m % 4)][:, :HALF], core.hT[:, m, 0:HALF], ALU.add)
                dve.tensor_tensor(core.hT[:, m, HALF:], core.ps[2 * (m % 4) + 1][:, :HALF], core.hT[:, m, HALF:],
                                  ALU.add).then_inc(added, 1)


def gate_up(nc, core, name, Wg, Wu, F, x, act_out):
    Gv, Uv = (W.rearrange("(k p) n -> p k n", p=P) for W in (Wg, Wu))
    NB = F // P
    assert NB % 2 == 0
    with Stage(nc, name) as st:
        w = [st.sb(f"w{i}", [P, KD, 2 * P]) for i in range(2)]
        sg = [st.sb(f"sg{i}", [P, 2, HALF]) for i in range(2)]
        w_in = [st.sem(f"w_in{i}") for i in range(2)]
        w_used, multiplied, silu_done, done = st.sem("w_used"), st.sem("multiplied"), st.sem("silu_done"), st.sem("done")
        block = st.open()

        def load(sp, n, j):
            sp.dma_start(w[j][:, :, 0:P], Gv[:, :, ds(n * P, P)]).then_inc(w_in[j], 16)
            sp.dma_start(w[j][:, :, P:], Uv[:, :, ds(n * P, P)]).then_inc(w_in[j], 16)

        @block.sync
        def _(sp):
            load(sp, 0, 0)
            load(sp, 1, 1)
            with sp.Fori(1, NB // 2) as i:
                for j in range(2):
                    sp.wait_ge(multiplied, i * 2 + (j - 1))
                    load(sp, i * 2 + j, j)

        @block.tensor
        def _(pe):
            with pe.Fori(0, NB // 2) as i:
                for j in range(2):
                    pe.wait_ge(w_in[j], i * 32 + 32)
                    pe.wait_ge(done, i * 2 + (j + 1))
                    for part in range(2):
                        for h, (t0, n) in enumerate(halves(T)):
                            for k in range(KD):
                                mm = pe.matmul(core.ps[4 * j + 2 * part + h][:, :n], w[j][:, k, part * P:(part + 1) * P],
                                               x[:, k, t0:t0 + n], start=(k == 0), stop=(k == KD - 1))
                    mm.then_inc(multiplied, 1)

        @block.scalar
        def _(act):
            with act.Fori(0, NB // 2) as i:
                for j in range(2):
                    act.wait_ge(multiplied, i * 2 + (j + 1))
                    act.wait_ge(done, i * 2 + (j + 1))
                    for h in range(2):
                        mm = act.activation(sg[j][:, h, :], core.ps[4 * j + h][:, :HALF], ACT.Silu)
                    mm.then_inc(silu_done, 1)

        @block.vector
        def _(dve):
            dve.sem_inc(done, 2)
            with dve.Fori(0, NB // 2) as i:
                for j in range(2):
                    dve.wait_ge(silu_done, i * 2 + (j + 1))
                    for h in range(2):
                        mm = dve.tensor_tensor(act_out[:, ds(i * 2 + j, 1), h * HALF:(h + 1) * HALF],
                                               core.ps[4 * j + 2 + h][:, :HALF], sg[j][:, h, :], ALU.mult)
                    mm.then_inc(done, 1)



def attend(nc, core, name, items):
    N = len(items)
    with Stage(nc, name) as st:
        prob = [st.sb(f"prob{i}", [P, 512]) for i in range(3)]
        probT = [st.sb(f"probT{i}", [P, 4, P]) for i in range(2)]
        top, shift, total, weight = (st.sb(x, [P, 8]) for x in ("top", "shift", "total", "weight"))
        scored, shifted, exped, turned, evacuated, valued, added = (
            st.sem(x) for x in ("scored", "shifted", "exped", "turned", "evacuated", "valued", "added"))
        S, PT, OB = core.ps[0:3], core.ps[3:5], core.ps[5:7]
        block = st.open()

        def tiles(n):
            return [(c, min(P, n - c * P)) for c in range(-(-n // P))]

        @block.tensor
        def _(pe):
            for step in range(N + 3):
                i = step
                if i < N:
                    it = items[i]
                    n = it["kT"].shape[1]
                    if i >= 3:
                        pe.wait_ge(exped, i - 2)
                    mm = pe.matmul(S[i % 3][:, :n], it["q"], it["kT"], start=True, stop=it["mask"] is None)
                    if it["mask"] is not None:
                        w = it["mask"].shape[1]
                        mm = pe.matmul(S[i % 3][:, n - w:n], core.ident[:, :], it["mask"], start=False, stop=True)
                    mm.then_inc(scored, 1)
                i = step - 2
                if 0 <= i < N:
                    n = items[i]["kT"].shape[1]
                    pe.wait_ge(exped, i + 1)
                    if i >= 2:
                        pe.wait_ge(evacuated, i - 1)
                    for c, m in tiles(n):
                        mm = pe.transpose(PT[i % 2][:m, c * P:(c + 1) * P], prob[i % 3][:, c * P:c * P + m], core.ident[:, :])
                    mm.then_inc(turned, 1)
                i = step - 3
                if 0 <= i < N:
                    n = items[i]["kT"].shape[1]
                    pe.wait_ge(evacuated, i + 1)
                    if i >= 2:
                        pe.wait_ge(added, i - 1)
                    for c, m in tiles(n):
                        mm = pe.matmul(OB[i % 2][:, :HD], probT[i % 2][:m, c, :], items[i]["v"][c],
                                       start=(c == 0), stop=(c == len(tiles(n)) - 1))
                    mm.then_inc(valued, 1)

        @block.vector
        def _(dve):
            for step in range(N + 3):
                i = step
                if i < N:
                    n, r = items[i]["kT"].shape[1], i % 8
                    dve.wait_ge(scored, i + 1)
                    dve.reduce_max(top[:, r:r + 1], S[i % 3][:, :n], AX_X)
                    dve.drain()
                    dve.tensor_scalar(shift[:, r:r + 1], top[:, r:r + 1], -SCALE, -SCALE * NEG * 1e-5,
                                      ALU.mult, ALU.min).then_inc(shifted, 1)
                i = step - 3
                if 0 <= i < N:
                    it, r = items[i], i % 8
                    dve.wait_ge(valued, i + 1)
                    dve.tensor_scalar(total[:, r:r + 1], total[:, r:r + 1], 1e-30, None, ALU.max)
                    dve.drain()
                    dve.reciprocal(weight[:, r:r + 1], total[:, r:r + 1])
                    dve.drain()
                    if it["gate"] is not None:
                        dve.tensor_tensor(weight[:, r:r + 1], weight[:, r:r + 1], it["gate"], ALU.mult)
                        dve.drain()
                    if it["first"]:
                        dve.tensor_scalar(it["out"], OB[i % 2][:, :HD], weight[:, r:r + 1], None, ALU.mult).then_inc(added, 1)
                    else:
                        dve.scalar_tensor_tensor(out=it["out"], in0=OB[i % 2][:, :HD], scalar=weight[:, r:r + 1],
                                                 in1=it["out"], op0=ALU.mult, op1=ALU.add).then_inc(added, 1)

        @block.scalar
        def _(act):
            for step in range(N + 2):
                i = step
                if i < N:
                    n, r = items[i]["kT"].shape[1], i % 8
                    act.wait_ge(shifted, i + 1)
                    if i >= 3:
                        act.wait_ge(turned, i - 2)
                    act.activation(prob[i % 3][:, :n], S[i % 3][:, :n], ACT.Exp, bias=shift[:, r:r + 1], scale=SCALE,
                                   accum_out=total[:, r:r + 1]).then_inc(exped, 1)
                i = step - 2
                if 0 <= i < N:
                    n = items[i]["kT"].shape[1]
                    act.wait_ge(turned, i + 1)
                    if i >= 2:
                        act.wait_ge(valued, i - 1)
                    m = min(n, P)
                    act.activation(probT[i % 2][:m, :-(-n // P), :],
                                   PT[i % 2][:m, :].rearrange("p (c q) -> p c q", q=P)[:, :-(-n // P), :],
                                   ACT.Copy).then_inc(evacuated, 1)


def memory_items(qmT, memkT, memv, onat):
    items = []
    for t in range(NT):
        for h in range(NG):
            o = (h % 2) * HD
            items.append(dict(q=qmT[o:o + HD, h // 2, t * P:(t + 1) * P], kT=memkT[o:o + HD, h // 2, :], mask=None,
                              v=[memv[:, m, GW + h * HD:GW + (h + 1) * HD] for m in range(MEM // P)],
                              gate=None, out=onat[:, t, CONV + h * HD:CONV + (h + 1) * HD], first=True))
    return items


def turn_outputs(nc, core, name, onat, mixT, blocks):
    with Stage(nc, name) as st:
        turned, copied = st.sem("turned"), st.sem("copied")
        block = st.open()

        @block.tensor
        def _(pe):
            for i, b in enumerate(blocks):
                for t in range(NT):
                    mm = pe.transpose(core.ps[i][:, t * P:(t + 1) * P], onat[:, t, b * P:(b + 1) * P], core.ident[:, :])
                mm.then_inc(turned, 1)

        @block.vector
        def _(dve):
            for i, b in enumerate(blocks):
                dve.wait_ge(turned, i + 1)
                dve.tensor_copy(mixT[:, b, :TP], core.ps[i][:, :])



def sample_memory(nc, core, A, l, qmT, mixT):
    NB2, MT = DB // 2, MEM // P
    with Stage(nc, f"smem{l}") as st:
        kraw = st.sb("kraw", [P, DB, MT, GW])
        vraw = st.sb("vraw", [P, DB, MT, GW])
        qbd = st.sb("qbd", [P, DB * 2, 32])
        kT = [st.sb(f"kT{i}", [P, 4, MEM]) for i in range(2)]
        prob = st.sb("prob", [P, NB2, MEM])
        probT = [st.sb(f"probT{i}", [P, MT, P]) for i in range(2)]
        top, shift, total, weight = (st.sb(x, [P, NB2]) for x in ("top", "shift", "total", "weight"))
        k_in, v_in = ([st.sem(f"{x}_in{i}") for i in range(2)] for x in "kv")
        q_ready = st.sem("q_ready")
        k_turned, k_copied, scored, shifted, exped = (st.sem(x) for x in ("k_turned", "k_copied", "scored", "shifted", "exped"))
        weighted, p_turned, p_copied, valued = (st.sem(x) for x in ("weighted", "p_turned", "p_copied", "valued"))
        block = st.open()

        @block.sync
        def _(sp):
            for i in range(2):
                b0 = i * DB // 2
                sp.dma_start(kraw[:, b0:b0 + DB // 2], A["cache_mem_k"][l, b0:b0 + DB // 2].rearrange(
                    "b (p c) h d -> p b (c h d)", c=MT).rearrange("p b (c w) -> p b c w", c=MT)).then_inc(k_in[i], 16)
            for i in range(2):
                b0 = i * DB // 2
                sp.dma_start(vraw[:, b0:b0 + DB // 2], A["cache_mem_v"][l, b0:b0 + DB // 2].rearrange(
                    "b (p c) h d -> p b (c h d)", c=MT).rearrange("p b (c w) -> p b c w", c=MT)).then_inc(v_in[i], 16)

        @block.gpsimd
        def _(pool):
            pool.memset(qbd[:, :, :], 0.0)
            pool.drain()
            for hp in range(2):
                for h2 in range(2):
                    o = h2 * HD
                    mm = pool.tensor_copy(
                        qbd[o:o + HD, :, :].rearrange("p (b hp) r -> p b hp r", hp=2)[:, :, hp, h2 * DS:(h2 + 1) * DS],
                        qmT[o:o + HD, hp, TP:].rearrange("p (b s) -> p b s", s=DS))
                    mm.then_inc(q_ready, 1)

        @block.tensor
        def _(pe):
            def scores(i):
                pe.wait_ge(k_in[2 * i // (DB // 2)], 16)
                for u in range(4):
                    b, hp = 2 * i + u // 2, u % 2
                    if u % 2 == 0 and (i or u // 2):
                        pe.wait_ge(k_copied, 2 * i + u // 2 - 1 if (2 * i + u // 2) >= 2 else 1)
                    for c in range(MT):
                        mm = pe.transpose(core.ps[u // 2][:, (u % 2) * MEM + c * P:(u % 2) * MEM + (c + 1) * P],
                                          kraw[:, b, c, hp * P:(hp + 1) * P], core.ident[:, :])
                    if u % 2:
                        mm.then_inc(k_turned, 1)
                pe.wait_ge(k_copied, 2 * (i + 1))
                pe.wait_ge(q_ready, 4)
                if i >= 2:
                    pe.wait_ge(exped, i - 1)
                for u in range(4):
                    mm = pe.matmul(core.ps[2 + i % 2][32 * u:32 * u + 32, :MEM], qbd[:, 4 * i + u, :], kT[i % 2][:, u, :],
                                   start=True, stop=True)
                mm.then_inc(scored, 1)

            def values(i):
                pe.wait_ge(weighted, i + 1)
                if i >= 1:
                    pe.wait_ge(p_copied, i)
                for c in range(MT):
                    mm = pe.transpose(core.ps[4][:, c * P:(c + 1) * P], prob[:, i, c * P:(c + 1) * P], core.ident[:, :])
                mm.then_inc(p_turned, 1)
                pe.wait_ge(p_copied, i + 1)
                pe.wait_ge(v_in[2 * i // (DB // 2)], 16)
                for u in range(4):
                    b, hp = 2 * i + u // 2, u % 2
                    for c in range(MT):
                        mm = pe.matmul(core.ps[5][:, (4 * i + u) * 32 % 512:(4 * i + u) * 32 % 512 + 32],
                                       vraw[:, b, c, hp * P:(hp + 1) * P], probT[i % 2][:, c, 32 * u:32 * u + 32],
                                       start=(c == 0), stop=(c == MT - 1))
                mm.then_inc(valued, 1)

            for i in range(NB2):
                scores(i)
                if i >= 1:
                    values(i - 1)
            values(NB2 - 1)

        @block.vector
        def _(dve):
            for i in range(NB2):
                for j in range(2):
                    dve.wait_ge(k_turned, 2 * i + j + 1)
                    if i >= 2:
                        dve.wait_ge(scored, i - 1)
                    dve.tensor_copy(kT[i % 2][:, 2 * j:2 * j + 2, :].rearrange("p u m -> p (u m)"), core.ps[j][:, :]).then_inc(k_copied, 1)
                dve.wait_ge(scored, i + 1)
                dve.reduce_max(top[:, i:i + 1], core.ps[2 + i % 2][:, :MEM], AX_X)
                dve.drain()
                dve.tensor_scalar(shift[:, i:i + 1], top[:, i:i + 1], -SCALE, None, ALU.mult).then_inc(shifted, 1)
                dve.wait_ge(exped, i + 1)
                dve.reciprocal(weight[:, i:i + 1], total[:, i:i + 1])
                dve.drain()
                dve.tensor_scalar(prob[:, i, :], prob[:, i, :], weight[:, i:i + 1], None, ALU.mult).then_inc(weighted, 1)

            dve.wait_ge(valued, NB2)
            for hp in range(2):
                for h2 in range(2):
                    o = h2 * HD
                    dve.tensor_copy(mixT[o:o + HD, KC + hp, TP:].rearrange("p (b s) -> p b s", s=DS),
                                    core.ps[5][o:o + HD, :].rearrange("p (b hp r) -> p b hp r", hp=2, r=32)[
                                        :, :, hp, h2 * DS:(h2 + 1) * DS])

        @block.scalar
        def _(act):
            for i in range(NB2):
                act.wait_ge(shifted, i + 1)
                act.activation(prob[:, i, :], core.ps[2 + i % 2][:, :MEM], ACT.Exp, bias=shift[:, i:i + 1], scale=SCALE,
                               accum_out=total[:, i:i + 1]).then_inc(exped, 1)
                act.wait_ge(p_turned, i + 1)
                if i >= 2:
                    act.wait_ge(valued, i - 1)
                act.activation(probT[i % 2][:, :, :].rearrange("p c q -> p (c q)"), core.ps[4][:, :MEM], ACT.Copy).then_inc(p_copied, 1)




def kv_project(nc, core, A, O, hn, kvn, kT):
    W = A["w_kv"].rearrange("(k p) n -> p k n", p=P)
    names = ("cmp_k", "cmp_v", "sel_k", "sel_v", "win_k", "win_v")
    rows = [P] * NT + [TS]
    with Stage(nc, "kv") as st:
        w = [st.sb(f"w{i}", [P, KD, 2 * GW]) for i in range(3)]
        w_in = [st.sem(f"w_in{i}") for i in range(3)]
        projected, copied, turned, k_copied, stored = (st.sem(x) for x in ("projected", "copied", "turned", "k_copied", "stored"))
        block = st.open()

        @block.sync
        def _(sp):
            for n in range(3):
                sp.dma_start(w[n][:, :, :], W[:, :, n * 2 * GW:(n + 1) * 2 * GW]).then_inc(w_in[n], 16)
            stores = 0
            for x in "kv":
                sp.dma_start(O[f"win_{x}_s"][:, 0:WIN - DS], A[f"state_win_{x}"][:, DS:]).then_inc(stored, 16)
                stores += 1
            for n in range(3):
                sp.wait_ge(copied, (NT + 1) * (n + 1))
                for i in range(2):
                    name, c0 = names[2 * n + i], (2 * n + i) * GW
                    sp.dma_start(O[f"{name}_p"][0].rearrange("(t p) h d -> p t (h d)", p=P), kvn[:, 0:NT, c0:c0 + GW]).then_inc(stored, 16)
                    stores += 1
                    if n < 2:
                        sp.dma_start(O[f"{name}_s"].rearrange("b s h d -> (b s) (h d)"), kvn[:TS, NT, c0:c0 + GW]).then_inc(stored, 16)
                        stores += 1
                    else:
                        for b in range(DB):
                            sp.dma_start(O[f"{name}_s"][b, WIN - DS:].rearrange("s h d -> s (h d)"),
                                         kvn[b * DS:(b + 1) * DS, NT, c0:c0 + GW]).then_inc(stored, 16)
                            stores += 1
            sp.wait_ge(stored, 16 * stores)

        @block.tensor
        def _(pe):
            for n in range(3):
                pe.wait_ge(w_in[n], 16)
                for t in range(NT + 1):
                    i = n * (NT + 1) + t
                    if i >= 6:
                        pe.wait_ge(copied, i - 5)
                    for k in range(KD):
                        mm = pe.matmul(core.ps[i % 6][:rows[t], :], hn[:, k, t * P:t * P + rows[t]], w[n][:, k, :],
                                       start=(k == 0), stop=(k == KD - 1))
                    mm.then_inc(projected, 1)
            for i, (x, gp) in enumerate(((0, 0), (0, 1), (1, 0), (1, 1))):
                pe.wait_ge(copied, (NT + 1) * (x + 2))
                if i >= 1:
                    pe.wait_ge(k_copied, 2 * i)
                for t in range(NT + 1):
                    mm = pe.transpose(core.ps[6 + t // NT][:, (t % NT) * P:(t % NT) * P + rows[t]],
                                      kvn[:rows[t], t, (2 + 2 * x) * GW + gp * P:(2 + 2 * x) * GW + (gp + 1) * P],
                                      core.ident[:rows[t], :rows[t]])
                mm.then_inc(turned, 1)

        @block.vector
        def _(dve):
            for i in range(3 * (NT + 1)):
                n, t = divmod(i, NT + 1)
                dve.wait_ge(projected, i + 1)
                dve.tensor_copy(kvn[:rows[t], t, n * 2 * GW:(n + 1) * 2 * GW], core.ps[i % 6][:rows[t], :]).then_inc(copied, 1)
            for i, (x, gp) in enumerate(((0, 0), (0, 1), (1, 0), (1, 1))):
                dve.wait_ge(turned, i + 1)
                dve.tensor_copy(kT[x][:, gp, :TP], core.ps[6][:, :]).then_inc(k_copied, 1)
                dve.tensor_copy(kT[x][:, gp, TP:], core.ps[7][:, :TS]).then_inc(k_copied, 1)


def query_project(nc, core, A, hn, qT, qmT, gates):
    W = A["w_in_b"][0].rearrange("(k p) n -> p k n", p=P)
    NQ, NGATE = NH * HD, 3 * NH
    parts = ((0, NQ // 2), (NQ // 2, NQ // 2), (NQ, NGATE + GW))
    rows = [P] * NT + [TS]
    with Stage(nc, "query") as st:
        w = [st.sb(f"w{i}", [P, KD, n]) for i, (_, n) in enumerate(parts)]
        w_in = [st.sem(f"w_in{i}") for i in range(3)]
        projected, copied, gated = st.sem("projected"), st.sem("copied"), st.sem("gated")
        block = st.open()
        blocks = [(gp, j) for gp in range(2) for j in range(NJ)] + [(2, 0), (2, 1)]

        @block.sync
        def _(sp):
            for i, (c0, n) in enumerate(parts[:2]):
                for g in range(2):
                    for j in range(NJ):
                        sp.dma_start(w[i][:, :, (2 * j + g) * HD:(2 * j + g + 1) * HD],
                                     W[:, :, c0 + (g * NJ + j) * HD:c0 + (g * NJ + j + 1) * HD]).then_inc(w_in[i], 16)
            sp.dma_start(w[2][:, :, :], W[:, :, parts[2][0]:]).then_inc(w_in[2], 16)

        @block.tensor
        def _(pe):
            for i, (part, j) in enumerate(blocks):
                pe.wait_ge(w_in[part], 16 * (2 * NJ if part < 2 else 1))
                if i >= 3:
                    pe.wait_ge(copied, i - 2)
                for h, (t0, n) in enumerate(halves(T)):
                    for k in range(KD):
                        if part < 2:
                            lhsT = w[part][:, k, j * P:(j + 1) * P]
                        else:
                            lhsT = w[2][:, k, NGATE + j * P:NGATE + (j + 1) * P]
                        mm = pe.matmul(core.ps[2 * (i % 3) + h][:, :n], lhsT, hn[:, k, t0:t0 + n],
                                       start=(k == 0), stop=(k == KD - 1))
                mm.then_inc(projected, 1)
            for t in range(NT + 1):
                for k in range(KD):
                    mm = pe.matmul(core.ps[6][:rows[t], t * NGATE:(t + 1) * NGATE], hn[:, k, t * P:t * P + rows[t]],
                                   w[2][:, k, :NGATE], start=(k == 0), stop=(k == KD - 1))
            mm.then_inc(gated, 1)

        @block.vector
        def _(dve):
            for i, (part, j) in enumerate(blocks):
                dve.wait_ge(projected, i + 1)
                out = qT[:, part * NJ + j, :] if part < 2 else qmT[:, j, :]
                dve.tensor_copy(out[:, :HALF], core.ps[2 * (i % 3)][:, :HALF])
                dve.tensor_copy(out[:, HALF:], core.ps[2 * (i % 3) + 1][:, :HALF]).then_inc(copied, 1)

        @block.scalar
        def _(act):
            act.wait_ge(gated, 1)
            act.activation(gates[:, 0:NT, :], core.ps[6][:, :NT * NGATE].rearrange("p (t g) -> p t g", g=NGATE), ACT.Sigmoid)
            act.activation(gates[:TS, NT, :], core.ps[6][:TS, NT * NGATE:(NT + 1) * NGATE], ACT.Sigmoid)



def load_compression(nc, core, A, w1, w2, bias):
    CP = CH // 2
    with Stage(nc, "cmpw") as st:
        pe_rows, peT = st.sb("pe_rows", [CH, 2, P]), st.sb("peT", [P, 2, CH])
        loaded, turned, copied, summed = (st.sem(x) for x in ("loaded", "turned", "copied", "summed"))
        block = st.open()

        @block.sync
        def _(sp):
            for x in range(2):
                for half in range(2):
                    sp.dma_start(w1[x][:, :, half * HD:(half + 1) * HD],
                                 A["cmp_w1"][x, half * CH:(half + 1) * CH].rearrange("(a c) d h -> (c d) a h", c=2)).then_inc(loaded, 16)
                sp.dma_start(w2[x][:, :], A["cmp_w2"][x]).then_inc(loaded, 16)
                sp.dma_start(pe_rows[:, x, :], A["cmp_pe"][x].rearrange("(a c) d -> a (c d)", c=2)).then_inc(loaded, 16)

        @block.tensor
        def _(pe):
            pe.wait_ge(loaded, 16 * 8)
            for x in range(2):
                mm = pe.transpose(core.ps[0][:, x * CH:(x + 1) * CH], pe_rows[:, x, :], core.ident[:CH, :CH])
            mm.then_inc(turned, 1)
            pe.wait_ge(copied, 1)
            for x in range(2):
                for a in range(CH):
                    half, cp = divmod(a, CP)
                    mm = pe.matmul(core.ps[1][:HD, x:x + 1], w1[x][:, cp, half * HD:(half + 1) * HD], peT[:, x, a:a + 1],
                                   start=(a == 0), stop=(a == CH - 1))
            mm.then_inc(summed, 1)

        @block.vector
        def _(dve):
            dve.wait_ge(turned, 1)
            dve.tensor_copy(peT[:, :, :], core.ps[0][:, :2 * CH].rearrange("p (x a) -> p x a", x=2)).then_inc(copied, 1)
            dve.wait_ge(summed, 1)
            dve.tensor_copy(bias[:, :], core.ps[1][:HD, :2])


def compress(nc, core, name, NB, NTL, R, load, by_gpsimd, w1, w2, bias, kcT, vc):
    CP = CH // 2
    N = NTL * R
    units = [(b, x, gp) for b in range(NB) for x in range(2) for gp in range(2)]
    U, Q = len(units), CP // 2
    with Stage(nc, name) as st:
        raw = [st.sb(f"raw{i}", [R, NTL, CH * GW]) for i in range(2)]
        xT = [[st.sb(f"xT{i}{g}", [P, CP, N]) for g in range(2)] for i in range(2)]
        high = st.sb("high", [HD, 2, N])
        hid = st.sb("hid", [HD, 2, N])
        act_h = [st.sb(f"act_h{i}", [HD, 2, N]) for i in range(2)]
        raw_in = [st.sem(f"raw_in{i}") for i in range(2)]
        evac = [st.sem("evac_low"), st.sem("evac_high")]
        turned, hidden, high_done, summed, gelu_done, out_done, out_copied = (
            st.sem(x) for x in ("turned", "hidden", "high_done", "summed", "gelu_done", "out_done", "out_copied"))
        block = st.open()

        def loads(eng):
            for i in range(2 * NB):
                if i >= 2:
                    eng.wait_ge(turned, Q * 2 * (i - 1))
                load(eng, i // 2, i % 2, raw[i % 2], raw_in[i % 2])
        st.pool_dma = by_gpsimd
        (block.gpsimd if by_gpsimd else block.sync)(loads)

        @block.tensor
        def _(pe):
            for step in range(U + 2):
                u = step
                if u < U:
                    b, x, gp = units[u]
                    i = 2 * b + x
                    if gp == 0:
                        pe.wait_ge(raw_in[i % 2], 16 * NTL * (i // 2 + 1))
                    for q in range(Q):
                        n = u * Q + q
                        if n >= 2:
                            for g in range(2):
                                pe.wait_ge(evac[g], 2 * (n - 1))
                        for c in range(4):
                            for t in range(NTL):
                                tok = q * 4 + c
                                mm = pe.transpose(core.ps[2 * (n % 2) + c // 2][:, (c % 2) * 256 + t * R:(c % 2) * 256 + (t + 1) * R],
                                                  raw[i % 2][:, t, tok * GW + gp * P:tok * GW + (gp + 1) * P], core.ident[:R, :R])
                        mm.then_inc(turned, 1)
                u = step - 1
                if 0 <= u < U:
                    x = units[u][1]
                    for g in range(2):
                        pe.wait_ge(evac[g], 2 * Q * (u + 1))
                    if u >= 1:
                        pe.wait_ge(summed, 2 * u)
                    for g in range(2):
                        for cp in range(CP):
                            mm = pe.matmul(core.ps[4 + g][:, :N], w1[x][:, cp, :], xT[u % 2][g][:, cp, :], start=(cp == 0), stop=(cp == CP - 1))
                        mm.then_inc(hidden, 1)
                u = step - 2
                if 0 <= u < U:
                    b, x, gp = units[u]
                    if u >= 1:
                        pe.wait_ge(out_copied, u)
                    for g in range(2):
                        pe.wait_ge(gelu_done, 2 * u + g + 1)
                        if x == 0:
                            mm = pe.matmul(core.ps[6][g * HD:(g + 1) * HD, :N - 1], w2[x][:, :], act_h[u % 2][:, g, :N - 1], start=True, stop=True)
                        else:
                            for t in range(NTL):
                                n = R - (t == NTL - 1)
                                mm = pe.matmul(core.ps[6][:n, (2 * t + g) * HD:(2 * t + g + 1) * HD], act_h[u % 2][:, g, t * R:t * R + n],
                                               w2[x][:, :], start=True, stop=True)
                    mm.then_inc(out_done, 1)

        def evacuate(eng, copy, u, g):
            for q in range(Q):
                n = u * Q + q
                eng.wait_ge(turned, n + 1)
                if q == 0 and u >= 2:
                    eng.wait_ge(hidden, 2 * (u - 1))
                for c in range(2):
                    src = core.banks[g * HD:(g + 1) * HD, 2 * (n % 2):2 * (n % 2) + 2, c * 256:c * 256 + N]
                    copy(xT[u % 2][g][c * HD:(c + 1) * HD, 2 * q:2 * q + 2, :], src).then_inc(evac[g], 1)

        @block.vector
        def _(dve):
            for step in range(U + 2):
                if step < U:
                    evacuate(dve, dve.tensor_copy, step, 0)
                u = step - 1
                if 0 <= u < U:
                    for g in range(2):
                        dve.wait_ge(high_done, 2 * u + g + 1)
                        if u >= 1:
                            dve.wait_ge(gelu_done, 2 * u - 1 + g)
                        dve.tensor_tensor(hid[:, g, :N - 1], core.ps[4 + g][:HD, :N - 1], high[:, g, :N - 1], ALU.add).then_inc(summed, 1)
                u = step - 2
                if 0 <= u < U:
                    b, x, gp = units[u]
                    dve.wait_ge(out_done, u + 1)
                    if x == 0:
                        dve.tensor_copy(kcT[:, b, gp, :N - 1], core.ps[6][:, :N - 1]).then_inc(out_copied, 1)
                    else:
                        if NTL > 1:
                            dve.tensor_copy(vc[:R, b, 0:NTL - 1, gp * P:(gp + 1) * P],
                                            core.ps[6][:R, :(NTL - 1) * P].rearrange("p (t d) -> p t d", d=P))
                        dve.tensor_copy(vc[:R - 1, b, NTL - 1, gp * P:(gp + 1) * P],
                                        core.ps[6][:R - 1, (NTL - 1) * P:NTL * P]).then_inc(out_copied, 1)

        @block.scalar
        def _(act):
            for step in range(U + 1):
                if step < U:
                    evacuate(act, act.copy, step, 1)
                u = step - 1
                if 0 <= u < U:
                    x = units[u][1]
                    for g in range(2):
                        act.wait_ge(hidden, 2 * u + g + 1)
                        if u >= 1:
                            act.wait_ge(summed, 2 * u - 1 + g)
                        act.copy(high[:, g, :N - 1], core.ps[4 + g][HD:, 1:N]).then_inc(high_done, 1)
                    for g in range(2):
                        act.wait_ge(summed, 2 * u + g + 1)
                        if u >= 2:
                            act.wait_ge(out_done, u - 1)
                        act.activation(act_h[u % 2][:, g, :N - 1], hid[:, g, :N - 1], ACT.Gelu_apprx_tanh, bias=bias[:, x:x + 1]).then_inc(gelu_done, 1)


def prompt_heads(nc, core, j, qT, gates, kT, kvn, kcT, vc, causal, cmp_mask, onat, qj, gj, oj):
    with Stage(nc, "headj") as st:
        block = st.open()

        @block.vector
        def _(dve):
            for gp in range(2):
                dve.tensor_copy(qj[:, gp, :], qT[:, ds(j + gp * NJ, 1), :TP])
            dve.tensor_copy(gj[:, :, :, :], gates[:, 0:NT, :].rearrange("p t (g a b) -> p t g a b", g=NG, a=NJ)[:, :, :, ds(j, 1), :])
    items = []
    for t in range(NT):
        n = (t + 1) * P
        for g in range(NG):
            o, gp = (g % 2) * HD, g // 2
            q = qj[o:o + HD, gp, t * P:(t + 1) * P]
            out = oj[:, t, g * HD:(g + 1) * HD]
            items.append(dict(q=q, kT=kcT[o:o + HD, 0, gp, :TP // CH - 1], mask=cmp_mask[:, t, :TP // CH - 1],
                              v=[vc[:TP // CH - 1, 0, 0, g * HD:(g + 1) * HD]], gate=gj[:, t, g, 0:1], out=out, first=True))
            for x in range(2):
                items.append(dict(q=q, kT=kT[x][o:o + HD, gp, :n], mask=causal[:, :],
                                  v=[kvn[:, c, (3 + 2 * x) * GW + g * HD:(3 + 2 * x) * GW + (g + 1) * HD] for c in range(t + 1)],
                                  gate=gj[:, t, g, x + 1:x + 2], out=out, first=False))
    attend(nc, core, "nsa", items)
    with Stage(nc, "headout") as st:
        block = st.open()

        @block.vector
        def _(dve):
            for g in range(NG):
                dve.tensor_copy(onat[:, :, 0:CONV].rearrange("p t (h d) -> p t h d", d=HD)[:, :, ds(j + g * NJ, 1), :],
                                oj[:, :, g * HD:(g + 1) * HD])



ROWS = 2 * NJ * DS
QUAD = 4
NQUAD = PAST // (QUAD * P)


class Sample:

    def __init__(self, sb):
        self.qall = sb("s_qall", [P, 2 * DB, 32])
        self.gate_rows = sb("s_gate_rows", [P, DB // 2, 3])
        self.cmp_idx_all = sb("s_cmp_idx_all", [P, DB, 2], I32)
        self.sel_idx_all = sb("s_sel_idx_all", [P, DB, NQUAD], I32)
        self.same = sb("s_same", [P, P])
        self.win_mask = sb("s_win_mask", [P, QUAD, P])
        self.new_mask = sb("s_new_mask", [P, DS])
        self.q = sb("s_q", [P, 4, 32])
        self.gate = sb("s_gate", [P, 3])
        self.cmp_idx = sb("s_cmp_idx", [P, 4], I32)
        self.sel_idx = sb("s_sel_idx", [P, 2 * NQUAD], I32)
        self.knew = sb("s_knew", [P, 2, 2, 2 * DS])
        self.vnew = sb("s_vnew", [DS, 2, 2, GW])
        self.kcT = sb("s_kcT", [P, 2, 2, NCH])
        self.vc = sb("s_vc", [P, 2, 2, GW])
        self.blocked = sb("s_blocked", [P, NSEL])


def sample_setup(nc, core, A, gate_scratch, S, qT, gates):
    with Stage(nc, "ssetup") as st:
        pages_c = st.sb("pages_c", [P, DB, 2], I32)
        pages_s = st.sb("pages_s", [P, DB], I32)
        row_c, row_s = st.sb("row_c", [P, 1], I32), st.sb("row_s", [P, NQUAD], I32)
        zeroed, built, loaded, gates_out, gates_in = (st.sem(x) for x in ("zeroed", "built", "loaded", "gates_out", "gates_in"))
        block = st.open()

        @block.sync
        def _(sp):
            sp.dma_start(S.same[:, :], A["c_same"]).then_inc(loaded, 16)
            sp.dma_start(S.win_mask[:, :, :], A["c_win_mask"]).then_inc(loaded, 16)
            sp.dma_start(S.new_mask[:, :], A["c_new_mask"]).then_inc(loaded, 16)
            sp.dma_start(row_c[:, :], A["c_cmp_row"]).then_inc(loaded, 16)
            sp.dma_start(row_s[:, :], A["c_sel_row"]).then_inc(loaded, 16)
            with nc.allow_non_contiguous_dma(reason="a few page numbers"):
                for t in range(2):
                    for pg in range(16):
                        sp.dma_start(pages_c[pg * 8:(pg + 1) * 8, :, t:t + 1].rearrange("p b o -> p (b o)"),
                                     A["page_table"][:, t * 16 + pg:t * 16 + pg + 1].rearrange("b o -> o b").to_broadcast([8, DB])).then_inc(loaded, 16)
                for pg in range(32):
                    sp.dma_start(pages_s[pg * 4:(pg + 1) * 4, :],
                                 A["page_table"][:, pg:pg + 1].rearrange("b o -> o b").to_broadcast([4, DB])).then_inc(loaded, 16)
            sp.dma_start(gate_scratch, gates[:TS, NT, :]).then_inc(gates_out, 16)
            sp.wait_ge(gates_out, 16)
            sp.wait_ge(zeroed, 1)
            for b in range(DB):
                for gp in range(2):
                    u = (b % 2) * 2 + gp
                    for gj in range(2 * NJ):
                        sp.dma_start(S.gate_rows[u * 32 + gj * DS:u * 32 + (gj + 1) * DS, b // 2, :],
                                     gate_scratch[b * DS:(b + 1) * DS, (gp * 6 + gj) * 3:(gp * 6 + gj + 1) * 3]).then_inc(gates_in, 16)
            sp.wait_ge(gates_in, 16 * DB * 2 * 2 * NJ)

        @block.gpsimd
        def _(pool):
            pool.memset(S.gate_rows[:, :, :], 0.0).then_inc(zeroed, 1)
            pool.memset(S.qall[:, :, :], 0.0)
            pool.drain()
            for gp in range(2):
                for g in range(2):
                    for j in range(NJ):
                        o, r = g * HD, (g * NJ + j) * DS
                        pool.tensor_copy(S.qall[o:o + HD, :, :].rearrange("p (b gp) r -> p b gp r", gp=2)[:, :, gp, r:r + DS],
                                         qT[o:o + HD, gp * NJ + j, TP:].rearrange("p (b s) -> p b s", s=DS)).then_inc(built, 1)
            pool.wait_ge(built, 4 * NJ)

        @block.vector
        def _(dve):
            dve.wait_ge(loaded, 16 * (5 + 32 + 32))
            for b in range(DB):
                dve.tensor_scalar(S.cmp_idx_all[:, b, :], pages_c[:, b, :], 8, row_c[:, 0:1], ALU.mult, ALU.add)
                dve.tensor_scalar(S.sel_idx_all[:, b, :], row_s[:, :], 0, None, ALU.add)
            dve.drain()
            for b in range(DB):
                for q in range(NQUAD):
                    dve.tensor_scalar(S.sel_idx_all[:, b, q:q + 1], pages_s[:, b:b + 1], 32, row_s[:, q:q + 1], ALU.mult, ALU.add)


def sample_pick(nc, core, O, S, i, kT):
    with Stage(nc, "pick") as st:
        loaded = st.sem("loaded")
        block = st.open()

        @block.sync
        def _(sp):
            for b in range(2):
                sp.dma_start(S.vnew[:, b, 0, :], O["sel_v_s"][ds(i * 2 + b, 1)].rearrange("o s h d -> (o s) (h d)")).then_inc(loaded, 16)
                sp.dma_start(S.vnew[:, b, 1, :], O["win_v_s"][ds(i * 2 + b, 1), WIN - DS:].rearrange("o s h d -> (o s) (h d)")).then_inc(loaded, 16)
            sp.wait_ge(loaded, 64)

        @block.vector
        def _(dve):
            dve.tensor_copy(S.q[:, :, :], S.qall[:, ds(i * 4, 4), :])
            dve.tensor_copy(S.gate[:, :], S.gate_rows[:, ds(i, 1), :].rearrange("p o x -> p (o x)"))
            dve.tensor_copy(S.cmp_idx[:, :], S.cmp_idx_all.rearrange("p b t -> p (b t)")[:, ds(i * 4, 4)])
            dve.tensor_copy(S.sel_idx[:, :], S.sel_idx_all.rearrange("p b t -> p (b t)")[:, ds(i * 2 * NQUAD, 2 * NQUAD)])
            for x in range(2):
                dve.tensor_copy(S.knew[:, x, :, :], kT[x][:, :, ds(i * 2 * DS + TP, 2 * DS)])


def sample_compressed(nc, core, S):
    N = NCH - 1
    acc = core.ps[7]
    with Stage(nc, "scmp") as st:
        prob, gated = st.sb("prob", [P, NCH]), st.sb("gated", [P, NCH])
        probT = st.sb("probT", [P, 2, P])
        stat = st.sb("stat", [P, 4])
        half = st.sb("half", [P, NCH + 1])
        chunk = st.sb("chunk", [P, NCH])
        score = [st.sb(f"score{i}", [P, NSEL + 1]) for i in range(3)]
        best = [st.sb(f"best{i}", [P, 8]) for i in range(2)]
        scored, shifted, exped, normed, summed, weighted, turned, copied = (
            st.sem(x) for x in ("scored", "shifted", "exped", "normed", "summed", "weighted", "turned", "copied"))
        block = st.open()

        @block.tensor
        def _(pe):
            for u in range(4):
                mm = pe.matmul(core.ps[0][32 * u:32 * u + 32, :N], S.q[:, u, :], S.kcT[:, u // 2, u % 2, :N], start=True, stop=True)
            mm.then_inc(scored, 1)
            pe.wait_ge(normed, 1)
            pe.matmul(core.ps[1][:, :N], S.same[:, :], prob[:, :N], start=True, stop=True).then_inc(summed, 1)
            pe.wait_ge(weighted, 1)
            for c in range(2):
                n = P - c
                mm = pe.transpose(core.ps[2][:n, c * P:(c + 1) * P], gated[:, c * P:c * P + n], core.ident[:, :])
            mm.then_inc(turned, 1)
            pe.wait_ge(copied, 1)
            for u in range(4):
                for c in range(2):
                    n = P - c
                    pe.matmul(acc[:, 32 * u:32 * u + 32], S.vc[:n, u // 2, c, (u % 2) * P:(u % 2 + 1) * P],
                              probT[:n, c, 32 * u:32 * u + 32], start=(u == 0 and c == 0), stop=False, skip_group_check=True)

        @block.scalar
        def _(act):
            act.wait_ge(shifted, 1)
            act.activation(prob[:, :N], core.ps[0][:, :N], ACT.Exp, bias=stat[:, 1:2], scale=SCALE, accum_out=stat[:, 2:3]).then_inc(exped, 1)
            act.wait_ge(turned, 1)
            act.copy(probT[:, 0, :], core.ps[2][:, :P])
            act.copy(probT[:P - 1, 1, :], core.ps[2][:P - 1, P:2 * P]).then_inc(copied, 1)

        @block.vector
        def _(dve):
            dve.memset(half[:, :], 0.0)
            dve.memset(score[0][:, NSEL:], -7.0)
            dve.wait_ge(scored, 1)
            dve.reduce_max(stat[:, 0:1], core.ps[0][:, :N], AX_X)
            dve.drain()
            dve.tensor_scalar(stat[:, 1:2], stat[:, 0:1], -SCALE, None, ALU.mult).then_inc(shifted, 1)
            dve.wait_ge(exped, 1)
            dve.reciprocal(stat[:, 3:4], stat[:, 2:3])
            dve.drain()
            dve.tensor_scalar(prob[:, :N], prob[:, :N], stat[:, 3:4], None, ALU.mult).then_inc(normed, 1)
            dve.drain()
            dve.tensor_scalar(gated[:, :N], prob[:, :N], S.gate[:, 0:1], None, ALU.mult).then_inc(weighted, 1)
            dve.wait_ge(summed, 1)
            dve.tensor_copy(half[:, 1:NCH], core.ps[1][:, :N])
            dve.drain()
            dve.tensor_tensor(chunk[:, :], half[:, 1:], half[:, :NCH], ALU.add)
            dve.drain()
            dve.reduce_sum(score[0][:, :NSEL], chunk[:, :].rearrange("p (m c) -> p m c", c=SELB // CH), AX_X)
            dve.drain()
            dve.memset(score[0][:, 0:1], FORCE)
            dve.memset(score[0][:, NSEL - 1:NSEL], FORCE)
            dve.drain()
            dve.max(best[0][:, :], score[0][:, :NSEL])
            dve.drain()
            dve.match_replace(score[1][:, :], best[0][:, :], score[0][:, :], NEG)
            dve.drain()
            dve.max(best[1][:, :], score[1][:, :NSEL])
            dve.drain()
            dve.memset(best[1][:, 7:8], -7.0)
            dve.drain()
            dve.match_replace(score[2][:, :], best[1][:, :], score[1][:, :], NEG)
            dve.drain()
            dve.tensor_scalar(S.blocked[:, :], score[2][:, :NSEL], NEG / 10, NEG, ALU.is_gt, ALU.mult)


def sample_branch(nc, core, name, S, NQ, branch, load, by_gpsimd):
    acc = core.ps[7]
    W = NQ * QUAD * P
    RK, RV = min(2 * NQ, 6), min(2 * NQ, 8)
    with Stage(nc, name) as st:
        kraw = [st.sb(f"kraw{i}", [P, QUAD, GW]) for i in range(RK)]
        vraw = [st.sb(f"vraw{i}", [P, QUAD, GW]) for i in range(RV)]
        kq = [st.sb(f"kq{i}", [P, QUAD * P]) for i in range(3)]
        score = st.sb("score", [P, W + DS])
        probT = [st.sb(f"probT{i}", [P, QUAD, P]) for i in range(2)]
        newT = st.sb("newT", [DS, P])
        stat = st.sb("stat", [P, 4])
        k_in, v_in = [st.sem(f"k_in{i}") for i in range(RK)], [st.sem(f"v_in{i}") for i in range(RV)]
        k_turned, kq_copied = st.sem("k_turned"), [st.sem("kq_copied_v"), st.sem("kq_copied_a")]
        scored, masked, shifted, exped, weighted = (st.sem(x) for x in ("scored", "masked", "shifted", "exped", "weighted"))
        p_turned, p_copied, valued = st.sem("p_turned"), [st.sem("p_copied_v"), st.sem("p_copied_a")], st.sem("valued")
        new_copied = st.sem("new_copied")
        block = st.open()
        tiles = [(q, b) for q in range(NQ) for b in range(2)]

        def loads(eng):
            def load_v(i):
                if i >= RV:
                    eng.wait_ge(valued, i - RV + 1)
                load(eng, "v", *tiles[i], vraw[i % RV], v_in[i % RV])
            for i, (q, b) in enumerate(tiles):
                if i >= RK:
                    eng.wait_ge(k_turned, 2 * (i - RK + 1))
                load(eng, "k", q, b, kraw[i % RK], k_in[i % RK])
            for i in range(len(tiles)):
                load_v(i)
        st.pool_dma = by_gpsimd
        (block.gpsimd if by_gpsimd else block.sync)(loads)

        @block.tensor
        def _(pe):
            NU = 4 * NQ
            for step in range(NU + 2):
                n = step
                if n < NU:
                    q, b, gp = n // 4, n // 2 % 2, n % 2
                    i = 2 * q + b
                    pe.wait_ge(k_in[i % RK], 16 * (i // RK + 1))
                    if n >= 3:
                        pe.wait_ge(kq_copied[(n - 3) % 2], (n - 3) // 2 + 1)
                    for c in range(QUAD):
                        mm = pe.transpose(core.ps[n % 3][:, c * P:(c + 1) * P], kraw[i % RK][:, c, gp * P:(gp + 1) * P], core.ident[:, :])
                    mm.then_inc(k_turned, 1)
                n = step - 2
                if 0 <= n < NU:
                    q, u = n // 4, n % 4
                    pe.wait_ge(kq_copied[n % 2], n // 2 + 1)
                    if u == 0 and q >= 2:
                        pe.wait_ge(masked, q - 1)
                    pe.matmul(core.ps[3 + q % 2][32 * u:32 * u + 32, :], S.q[:, u, :], kq[n % 3][:, :], start=True, stop=True).then_inc(scored, 1)
            for u in range(4):
                mm = pe.matmul(core.ps[5][32 * u:32 * u + 32, :DS], S.q[:, u, :], S.knew[:, branch - 1, u % 2, (u // 2) * DS:(u // 2 + 1) * DS],
                               start=True, stop=True)
            mm.then_inc(scored, 1)
            pe.wait_ge(weighted, 1)
            pe.transpose(core.ps[6][:DS, :P], score[:, W:], core.ident[:, :]).then_inc(p_turned, 1)
            for step in range(NQ + 1):
                q = step
                if q < NQ:
                    if q >= 2:
                        pe.wait_ge(p_copied[q % 2], q // 2)
                    for c in range(QUAD):
                        mm = pe.transpose(core.ps[q % 2][:, c * P:(c + 1) * P], score[:, (q * QUAD + c) * P:(q * QUAD + c + 1) * P], core.ident[:, :])
                    mm.then_inc(p_turned, 1)
                q = step - 1
                if q < 0:
                    pe.wait_ge(new_copied, 1)
                    for u in range(4):
                        pe.matmul(acc[:, 32 * u:32 * u + 32], S.vnew[:, u // 2, branch - 1, (u % 2) * P:(u % 2 + 1) * P],
                                  newT[:, 32 * u:32 * u + 32], start=False, stop=False, skip_group_check=True)
                else:
                    pe.wait_ge(p_copied[q % 2], q // 2 + 1)
                    for b in range(2):
                        i = 2 * q + b
                        pe.wait_ge(v_in[i % RV], 16 * (i // RV + 1))
                        for c in range(QUAD):
                            for gp in range(2):
                                u = 2 * b + gp
                                mm = pe.matmul(acc[:, 32 * u:32 * u + 32], vraw[i % RV][:, c, gp * P:(gp + 1) * P],
                                               probT[q % 2][:, c, 32 * u:32 * u + 32], start=False, stop=False, skip_group_check=True)
                        mm.then_inc(valued, 1)

        def copy_key(eng, copy, n):
            eng.wait_ge(k_turned, n + 1)
            if n >= 3:
                eng.wait_ge(scored, n - 2)
            copy(kq[n % 3][:, :], core.ps[n % 3][:, :]).then_inc(kq_copied[n % 2], 1)

        def copy_prob(eng, copy, q):
            eng.wait_ge(p_turned, q + 2)
            if q >= 2:
                eng.wait_ge(valued, 2 * (q - 1))
            copy(probT[q % 2][:, :, :].rearrange("p c r -> p (c r)"), core.ps[q % 2][:, :]).then_inc(p_copied[q % 2], 1)

        @block.vector
        def _(dve):
            for q in range(NQ + 1):
                if q < NQ:
                    copy_key(dve, dve.tensor_copy, 4 * q)
                    copy_key(dve, dve.tensor_copy, 4 * q + 2)
                if q >= 1:
                    dve.wait_ge(scored, 4 * q)
                    out = score[:, (q - 1) * QUAD * P:q * QUAD * P]
                    if branch == 1:
                        mask = S.blocked[:, :].unsqueeze(1).unsqueeze(3).to_broadcast([P, QUAD, NSEL, 2])
                        dve.tensor_tensor(out.rearrange("p (c m o) -> p c m o", c=QUAD, o=2),
                                          core.ps[3 + (q - 1) % 2].rearrange("p (c m o) -> p c m o", c=QUAD, o=2), mask, ALU.add).then_inc(masked, 1)
                    else:
                        dve.tensor_tensor(out, core.ps[3 + (q - 1) % 2][:, :], S.win_mask[:, :, :].rearrange("p c k -> p (c k)"), ALU.add).then_inc(masked, 1)
            dve.wait_ge(scored, 4 * NQ + 1)
            dve.tensor_tensor(score[:, W:], core.ps[5][:, :DS], S.new_mask[:, :], ALU.add)
            dve.drain()
            dve.reduce_max(stat[:, 0:1], score[:, :], AX_X)
            dve.drain()
            dve.tensor_scalar(stat[:, 1:2], stat[:, 0:1], -SCALE, None, ALU.mult).then_inc(shifted, 1)
            dve.wait_ge(exped, 1)
            dve.reciprocal(stat[:, 3:4], stat[:, 2:3])
            dve.drain()
            dve.tensor_scalar(score[:, :], score[:, :], stat[:, 3:4], S.gate[:, branch:branch + 1], ALU.mult, ALU.mult).then_inc(weighted, 1)
            dve.wait_ge(p_turned, 1)
            dve.tensor_copy(newT[:, :], core.ps[6][:DS, :P]).then_inc(new_copied, 1)
            for q in range(0, NQ, 2):
                copy_prob(dve, dve.tensor_copy, q)

        @block.scalar
        def _(act):
            for n in range(1, 4 * NQ, 2):
                copy_key(act, act.copy, n)
            act.wait_ge(shifted, 1)
            act.activation(score[:, :], score[:, :], ACT.Exp, bias=stat[:, 1:2], scale=SCALE, accum_out=stat[:, 2:3]).then_inc(exped, 1)
            for q in range(1, NQ, 2):
                copy_prob(act, act.copy, q)


def sample_out(nc, core, S, i, mixT, tok):
    with Stage(nc, "sout") as st:
        block = st.open()

        @block.vector
        def _(dve):
            for gp in range(2):
                for g in range(2):
                    for j in range(NJ):
                        h, o, r = (2 * gp + g) * NJ + j, g * HD, (g * NJ + j) * DS
                        src = core.ps[7][o:o + HD, :P].rearrange("p (b gp r) -> p b gp r", b=2, gp=2)[:, :, gp, r:r + DS]
                        dst = tok[(h % 2) * HD:(h % 2 + 1) * HD, h // 2, :].rearrange("p (b s) -> p b s", b=2)
                        dve.tensor_copy(dst, src)
            dve.drain()
            dve.tensor_copy(mixT[:, 0:KC, ds(i * 2 * DS + TP, 2 * DS)], tok[:, :, :])


def sample_nsa(nc, core, A, O, gate_scratch, qT, gates, kT, w1, w2, bias, mixT):
    with ExitStack() as ctx:
        def sb(name, shape, dt=F32):
            return ctx.enter_context(nc.sbuf_tensor(name, shape, dt))
        S = Sample(sb)
        tok = sb("s_tok", [P, KC, 2 * DS])
        cmp_pool = [A[f"cache_cmp_{x}"].rearrange("n (r c) h d -> (n r) (c h d)", c=CH) for x in "kv"]
        sel_pool = {x: A[f"cache_sel_{x}"].rearrange("n (r c) h d -> (n r) (c h d)", c=QUAD) for x in "kv"}

        def gather(eng, out, pool, index, landed):
            eng.indirect_dma_start(out, None, pool, bass.IndirectOffsetOnAxis(index, 0)).then_inc(landed, 16)

        def load_chunks(eng, b, x, buf, landed):
            for t in range(2):
                gather(eng, buf[:, t, :], cmp_pool[x], S.cmp_idx[:, 2 * b + t:2 * b + t + 1], landed)

        def load_selected(eng, x, q, b, buf, landed):
            gather(eng, buf[:, :, :].rearrange("p c w -> p (c w)"), sel_pool[x], S.sel_idx[:, b * NQUAD + q:b * NQUAD + q + 1], landed)

        sample_setup(nc, core, A, gate_scratch, S, qT, gates)
        with nc.Fori(0, DB // 2) as i:
            def load_window(eng, x, q, b, buf, landed):
                eng.dma_start(buf[:, :, :].rearrange("p c w -> p (c w)"),
                              A[f"state_win_{x}"][ds(i * 2 + b, 1)].rearrange("o (p c) h d -> p (o c h d)", c=QUAD)).then_inc(landed, 16)
            sample_pick(nc, core, O, S, i, kT)
            compress(nc, core, "scompress", 2, 2, P, load_chunks, True, w1, w2, bias, S.kcT, S.vc)
            sample_compressed(nc, core, S)
            sample_branch(nc, core, "swin", S, 1, 2, load_window, False)
            sample_branch(nc, core, "ssel", S, NQUAD, 1, load_selected, True)
            sample_out(nc, core, S, i, mixT, tok)



def route(nc, core, A, hn, share):
    rows = [P] * NT + [TS]
    EXTRA = 6
    with Stage(nc, "route") as st:
        w, b = st.sb("w", [P, KD, NE]), st.sb("b", [P, NE])
        logit = st.sb("logit", [P, NT + 1, NE + EXTRA])
        left = st.sb("left", [P, NT + 1, NE + EXTRA])
        best = st.sb("best", [P, NT + 1, 8])
        e = st.sb("e", [P, NT + 1, NE])
        stat = st.sb("stat", [P, NT + 1, 3])
        shareT = st.sb("shareT", [NE, T])
        w_in, routed, shifted, exped, shared, turned, copied, spread, spread_copied = (st.sem(x) for x in (
            "w_in", "routed", "shifted", "exped", "shared", "turned", "copied", "spread", "spread_copied"))
        block = st.open()

        @block.sync
        def _(sp):
            sp.dma_start(w[:, :, :], A["w_router"][0].rearrange("(k p) e -> p k e", p=P)).then_inc(w_in, 16)
            sp.dma_start(b[:, :], A["b_router"].to_broadcast([P, NE])).then_inc(w_in, 16)

        @block.tensor
        def _(pe):
            pe.wait_ge(w_in, 32)
            for t in range(NT + 1):
                for k in range(KD):
                    mm = pe.matmul(core.ps[0][:rows[t], t * NE:(t + 1) * NE], hn[:, k, t * P:t * P + rows[t]], w[:, k, :],
                                   start=(k == 0), stop=(k == KD - 1))
            mm.then_inc(routed, 1)
            pe.wait_ge(shared, 1)
            for t in range(NT + 1):
                mm = pe.transpose(core.ps[1 + t // NT][:NE, (t % NT) * P:(t % NT) * P + rows[t]], e[:rows[t], t, :],
                                  core.ident[:rows[t], :rows[t]])
            mm.then_inc(turned, 1)
            pe.wait_ge(copied, 1)
            for x in range(NE):
                if x >= 2:
                    pe.wait_ge(spread_copied, x - 1)
                for h, (t0, n) in enumerate(halves(T)):
                    mm = pe.matmul(core.ps[4 + 2 * (x % 2) + h][:, :n], core.ident[:NE, x:x + 1].to_broadcast([NE, P]), shareT[:, t0:t0 + n],
                                   start=True, stop=True)
                mm.then_inc(spread, 1)

        @block.vector
        def _(dve):
            dve.memset(logit[:, :, :], 0.0)
            dve.memset(best[:, :, :], 0.0)
            dve.drain()
            dve.memset(logit[:, :, NE:], -2e38)
            dve.wait_ge(routed, 1)
            for t in range(NT + 1):
                dve.tensor_tensor(logit[:rows[t], t, :NE], core.ps[0][:rows[t], t * NE:(t + 1) * NE], b[:rows[t], :], ALU.add)
            dve.drain()
            for t in range(NT + 1):
                dve.max(best[:, t, :], logit[:, t, :NE])
            dve.drain()
            dve.memset(best[:, :, 2:], -2e38)
            dve.tensor_tensor(e[:, :, :], logit[:, :, :NE], best[:, :, 0:1].to_broadcast([P, NT + 1, NE]), ALU.subtract).then_inc(shifted, 1)
            dve.drain()
            for t in range(NT + 1):
                dve.match_replace(left[:, t, :], best[:, t, :], logit[:, t, :], NEG)
            dve.drain()
            dve.tensor_scalar(left[:, :, :NE], left[:, :, :NE], NEG / 10, None, ALU.is_lt)
            dve.drain()
            dve.wait_ge(exped, 1)
            dve.tensor_tensor(e[:, :, :], e[:, :, :], left[:, :, :NE], ALU.mult)
            dve.drain()
            dve.reduce_sum(stat[:, :, 0], e[:, :, :], AX_X)
            dve.drain()
            dve.reciprocal(stat[:, :, 1], stat[:, :, 0])
            dve.drain()
            dve.tensor_tensor(e[:, :, :], e[:, :, :], stat[:, :, 1:2].to_broadcast([P, NT + 1, NE]), ALU.mult).then_inc(shared, 1)
            dve.wait_ge(turned, 1)
            dve.tensor_copy(shareT[:, :TP], core.ps[1][:NE, :])
            dve.tensor_copy(shareT[:, TP:], core.ps[2][:NE, :TS]).then_inc(copied, 1)
            for x in range(NE):
                dve.wait_ge(spread, x + 1)
                for h, (t0, n) in enumerate(halves(T)):
                    mm = dve.tensor_copy(share[:, x, t0:t0 + n], core.ps[4 + 2 * (x % 2) + h][:, :n])
                mm.then_inc(spread_copied, 1)

        @block.scalar
        def _(act):
            act.wait_ge(shifted, 1)
            act.activation(e[:, :, :], e[:, :, :], ACT.Exp).then_inc(exped, 1)


def expert_hidden(nc, core, A, x, hn, share_x, hidden):
    Gv, Uv = (A[n][0, ds(x, 1)].rearrange("o (k p) n -> p (o k) n", p=P) for n in ("w_e_gate", "w_e_up"))
    NB = DEX // P
    with Stage(nc, "expert") as st:
        w = [st.sb(f"w{i}", [P, KD, 2 * P]) for i in range(3)]
        sg = [st.sb(f"sg{i}", [P, T]) for i in range(2)]
        w_in = [st.sem(f"w_in{i}") for i in range(3)]
        multiplied, silu_done, done = st.sem("multiplied"), st.sem("silu_done"), st.sem("done")
        block = st.open()

        @block.sync
        def _(sp):
            for n in range(NB):
                if n >= 3:
                    sp.wait_ge(multiplied, n - 2)
                sp.dma_start(w[n % 3][:, :, 0:P], Gv[:, :, n * P:(n + 1) * P]).then_inc(w_in[n % 3], 16)
                sp.dma_start(w[n % 3][:, :, P:], Uv[:, :, n * P:(n + 1) * P]).then_inc(w_in[n % 3], 16)

        @block.tensor
        def _(pe):
            for m in range(NB):
                pe.wait_ge(w_in[m % 3], 32 * (m // 3 + 1))
                if m >= 2:
                    pe.wait_ge(done, m - 1)
                for part in range(2):
                    for h, (t0, n) in enumerate(halves(T)):
                        for k in range(KD):
                            mm = pe.matmul(core.ps[4 * (m % 2) + 2 * part + h][:, :n], w[m % 3][:, k, part * P:(part + 1) * P],
                                           hn[:, k, t0:t0 + n], start=(k == 0), stop=(k == KD - 1))
                mm.then_inc(multiplied, 1)

        @block.scalar
        def _(act):
            for m in range(NB):
                act.wait_ge(multiplied, m + 1)
                if m >= 2:
                    act.wait_ge(done, m - 1)
                for h, (t0, n) in enumerate(halves(T)):
                    mm = act.activation(sg[m % 2][:, t0:t0 + n], core.ps[4 * (m % 2) + h][:, :n], ACT.Silu)
                mm.then_inc(silu_done, 1)

        @block.vector
        def _(dve):
            for m in range(NB):
                dve.wait_ge(silu_done, m + 1)
                dve.tensor_tensor(sg[m % 2][:, :], sg[m % 2][:, :], share_x, ALU.mult)
                dve.drain()
                for h, (t0, n) in enumerate(halves(T)):
                    mm = dve.tensor_tensor(hidden[:, m, t0:t0 + n], core.ps[4 * (m % 2) + 2 + h][:, :n], sg[m % 2][:, t0:t0 + n], ALU.mult)
                mm.then_inc(done, 1)


def final_norm(nc, core, O, hn):
    groups = [(t, k0) for t in range(NT + 1) for k0 in (0, 4)]
    rows = [P] * NT + [TS]
    with Stage(nc, "final") as st:
        out = st.sb("out", [P, NT + 1, D])
        turned, copied, stored = st.sem("turned"), st.sem("copied"), st.sem("stored")
        block = st.open()

        @block.tensor
        def _(pe):
            for n, (t, k0) in enumerate(groups):
                if n >= 8:
                    pe.wait_ge(copied, n - 7)
                for k in range(4):
                    mm = pe.transpose(core.ps[n % 8][:rows[t], k * P:(k + 1) * P], hn[:, k0 + k, t * P:t * P + rows[t]], core.ident[:, :])
                mm.then_inc(turned, 1)

        @block.vector
        def _(dve):
            for n, (t, k0) in enumerate(groups):
                dve.wait_ge(turned, n + 1)
                dve.tensor_copy(out[:rows[t], t, k0 * P:(k0 + 4) * P], core.ps[n % 8][:rows[t], :]).then_inc(copied, 1)

        @block.sync
        def _(sp):
            for t in range(NT):
                sp.wait_ge(copied, 2 * (t + 1))
                sp.dma_start(O["y_p"][0, t * P:(t + 1) * P, :], out[:, t, :]).then_inc(stored, 16)
            sp.wait_ge(copied, 2 * (NT + 1))
            sp.dma_start(O["y_s"].rearrange("b s d -> (b s) d"), out[:TS, NT, :]).then_inc(stored, 16)
            sp.wait_ge(stored, 16 * (NT + 1))


def build(nc, A, O, stop=99):
    with ExitStack() as ctx:
        core = Core(nc, ctx)

        def scope(stack):
            return lambda name, shape, dt=F32: stack.enter_context(nc.sbuf_tensor(name, shape, dt))
        mixT = core.sb("mixT", [P, KD, T])
        memv = [core.sb(f"memv{l}", [P, MEM // P, 2 * GW]) for l in range(2)]
        memkT = [core.sb(f"memkT{l}", [P, 2, MEM]) for l in range(2)]
        qmT = core.sb("qmT", [P, 2, T])
        load_tokens(nc, core, A)
        memory_kv(nc, core, A, O, memv, memkT)
        with ExitStack() as stack:
            sb = scope(stack)
            up_p = sb("up_p", [P, KC, TAIL + TP])
            up_s = sb("up_s", [P, KC, DB, TAIL + DS])
            convw = sb("convw", [P, KC, CW])
            with nc.sbuf_tensor("hn_0", [P, KD, T], F32) as hn:
                rms_norm(nc, core, "norm_mix0", "g_mix", 0, hn)
                conv_input(nc, core, A, O, hn, up_p, up_s, qmT, convw)
            y = sb("y", [P, KC, T])
            convolve(nc, core, up_p, up_s, convw, y)
            conv_norm(nc, core, y, mixT)
            onat = sb("onat_0", [P, NT, D])
            attend(nc, core, "pmem0", memory_items(qmT, memkT[0], memv[0], onat))
            turn_outputs(nc, core, "turn0", onat, mixT, [KC, KC + 1])
            sample_memory(nc, core, A, 0, qmT, mixT)
        if stop == 1:
            return
        add_product(nc, core, "wout0", A["w_out"][0], KD, mixT)
        with ExitStack() as stack:
            sb = scope(stack)
            hidden = sb("hidden", [P, DFF // P, T])
            hn = sb("hn_f", [P, KD, T])
            rms_norm(nc, core, "norm_ffn0", "g_ffn", 0, hn)
            gate_up(nc, core, "ffn", A["w_ff_gate"][0], A["w_ff_up"][0], DFF, hn, hidden)
            add_product(nc, core, "ffdown", A["w_ff_down"][0], DFF // P, hidden)
        if stop == 2:
            return
        with ExitStack() as layer:
            sb = scope(layer)
            kT = [sb(f"kT{x}", [P, 2, T]) for x in range(2)]
            qT = sb("qT", [P, 2 * NJ, T])
            gates = sb("gates", [P, NT + 1, 3 * NH])
            w1 = [sb(f"cw1_{x}", [P, CH // 2, 2 * HD]) for x in range(2)]
            w2 = [sb(f"cw2_{x}", [HD, HD]) for x in range(2)]
            bias = sb("cmp_bias", [HD, 2])
            with ExitStack() as stack:
                sb = scope(stack)
                kvn = sb("kvn", [P, NT + 1, 6 * GW])
                with nc.sbuf_tensor("hn_1", [P, KD, T], F32) as hn:
                    rms_norm(nc, core, "norm_kv", "g_kv", 0, hn)
                    kv_project(nc, core, A, O, hn, kvn, kT)
                    rms_norm(nc, core, "norm_mix1", "g_mix", KD, hn)
                    query_project(nc, core, A, hn, qT, qmT, gates)
                load_compression(nc, core, A, w1, w2, bias)
                onat = sb("onat_1", [P, NT, D])
                NCP = TP // CH
                kcT, vc = sb("kcT_p", [P, 1, 2, NCP]), sb("vc_p", [NCP, 1, 1, GW])
                causal, cmp_mask = sb("causal", [P, P]), sb("cmp_mask", [P, NT, NCP])
                qj, gj, oj = sb("qj", [P, 2, TP]), sb("gj", [P, NT, NG, 3]), sb("oj", [P, NT, GW])

                def load_chunks(eng, b, x, buf, landed):
                    src = O["cmp_k_p" if x == 0 else "cmp_v_p"][0].rearrange("(n c) h d -> n (c h d)", c=CH)
                    eng.dma_start(buf[:, 0, :], src).then_inc(landed, 16)
                with Stage(nc, "masks") as st:
                    masks_in = st.sem("masks_in")
                    block = st.open()

                    @block.sync
                    def _(sp):
                        sp.dma_start(causal[:, :], A["c_causal"]).then_inc(masks_in, 16)
                        sp.dma_start(cmp_mask[:, :, :], A["c_cmp_mask"]).then_inc(masks_in, 16)
                        sp.wait_ge(masks_in, 32)
                compress(nc, core, "pcmp", 1, 1, NCP, load_chunks, False, w1, w2, bias, kcT, vc)
                with nc.Fori(0, NJ) as j:
                    prompt_heads(nc, core, j, qT, gates, kT, kvn, kcT, vc, causal, cmp_mask, onat, qj, gj, oj)
                attend(nc, core, "pmem1", memory_items(qmT, memkT[1], memv[1], onat))
                turn_outputs(nc, core, "turn1", onat, mixT, list(range(KD)))
            if stop == 3:
                return
            sample_memory(nc, core, A, 1, qmT, mixT)
            gate_scratch = nc.dram_tensor("gate_scratch", (TS, 3 * NH), F32).ap()
            sample_nsa(nc, core, A, O, gate_scratch, qT, gates, kT, w1, w2, bias, mixT)
        if stop == 4:
            return
        add_product(nc, core, "wout1", A["w_out"][1], KD, mixT)
        with ExitStack() as stack:
            sb = scope(stack)
            hn = sb("hn_e", [P, KD, T])
            share, share_x = sb("share", [P, NE, T]), sb("share_x", [P, T])
            hidden = sb("hidden_e", [P, DEX // P, T])
            rms_norm(nc, core, "norm_ffn1", "g_ffn", KD, hn)
            route(nc, core, A, hn, share)
            with nc.Fori(0, NE) as x:
                with Stage(nc, "pickx") as st:
                    block = st.open()

                    @block.vector
                    def _(dve):
                        dve.tensor_copy(share_x[:, :], share[:, ds(x, 1), :].rearrange("p o t -> p (o t)"))
                expert_hidden(nc, core, A, x, hn, share_x[:, :], hidden)
                add_product(nc, core, "edown", A["w_e_down"][0, ds(x, 1)].rearrange("o f d -> (o f) d"), DEX // P, hidden)
            rms_norm(nc, core, "norm_final", "g_final", 0, hn)
            final_norm(nc, core, O, hn)


def shape_constants(np):
    q, t = np.arange(P), np.arange(NT)
    pos = t[None, :, None] * P + q[:, None, None]
    ends = np.arange(TP // CH)[None, None, :] * CH + 2 * CH - 1
    row = np.arange(P) % 32
    used, s = row < 24, row % DS
    key = np.arange(P)[None, :] * DS + np.arange(4)[:, None]
    same = (s[:, None] == s[None, :]) & (row[:, None] // 12 == row[None, :] // 12) & used[:, None] & used[None, :]
    same &= (np.arange(P)[:, None] // 32 == np.arange(P)[None, :] // 32)
    return {
        "c_ident": np.eye(P, dtype=np.float32),
        "c_causal": np.where(q[None, :] <= q[:, None], 0, NEG).astype(np.float32),
        "c_cmp_mask": np.where(ends <= pos, 0, NEG).astype(np.float32),
        "c_same": np.where(same, 0.5, 0).astype(np.float32),
        "c_win_mask": np.where(used[:, None, None] & (key[None] <= s[:, None, None]), NEG, 0).astype(np.float32),
        "c_new_mask": np.where(used[:, None] & (np.arange(DS)[None, :] > s[:, None]), NEG, 0).astype(np.float32),
        "c_cmp_row": (np.arange(P) % 8).astype(np.int32).reshape(P, 1),
        "c_sel_row": ((np.arange(P) % 4)[:, None] * 8 + np.arange(8)[None, :]).astype(np.int32),
    }


_INS = ["x_prompt", "x_sample", "cache_mem_k", "cache_mem_v", "state_conv", "cache_cmp_k", "cache_cmp_v",
        "cache_sel_k", "cache_sel_v", "state_win_k", "state_win_v", "page_table", "mem_prompt",
        "g_mix", "g_ffn", "g_mem", "w_mem_kv", "w_in_a", "conv_w", "conv_b", "ln_g", "ln_b", "w_in_b", "g_kv", "w_kv",
        "cmp_pe", "cmp_w1", "cmp_w2", "w_out", "w_ff_gate", "w_ff_up", "w_ff_down", "w_router", "b_router",
        "w_e_gate", "w_e_up", "w_e_down", "g_final"]
_OUTS = [("y_p", (1, TP, D)), ("y_s", (DB, DS, D)), ("mem_k_p", (2, 1, MEM, NG, HD)), ("mem_v_p", (2, 1, MEM, NG, HD)),
         ("conv_p", (1, 1, TAIL, CONV)), ("conv_s", (1, DB, TAIL, CONV)),
         ("cmp_k_p", (1, TP, NG, HD)), ("cmp_v_p", (1, TP, NG, HD)), ("sel_k_p", (1, TP, NG, HD)), ("sel_v_p", (1, TP, NG, HD)),
         ("cmp_k_s", (DB, DS, NG, HD)), ("cmp_v_s", (DB, DS, NG, HD)), ("sel_k_s", (DB, DS, NG, HD)), ("sel_v_s", (DB, DS, NG, HD)),
         ("win_k_p", (1, WIN, NG, HD)), ("win_v_p", (1, WIN, NG, HD)), ("win_k_s", (DB, WIN, NG, HD)), ("win_v_s", (DB, WIN, NG, HD))]


def kernel(**inputs):
    import numpy as np
    import concourse.bacc as bacc
    from concourse.bass_utils import run_bass_kernel_spmd

    nc = bacc.Bacc("TRN2", target_bir_lowering=False, num_devices=1)
    arrays, A, O = {}, {}, {}
    data = {name: np.ascontiguousarray(inputs[name]) for name in _INS} | shape_constants(np)
    for name, a in data.items():
        arrays[f"in_{name}"] = a
        A[name] = nc.dram_tensor(f"in_{name}", a.shape, mybir.dt.from_np(a.dtype), kind="ExternalInput").ap()
    for name, shape in _OUTS:
        O[name] = nc.dram_tensor(f"out_{name}", shape, F32, kind="ExternalOutput").ap()
    build(nc, A, O)
    r = run_bass_kernel_spmd(nc, [arrays], core_ids=[0])
    return tuple(r.results[0][f"out_{name}"] for name, _ in _OUTS)
```
